# Optimizing a Trainium2 kernel written in Bass

```python
import math
import jax, jax.numpy as jnp
from jax import lax
import numpy as np

D_MODEL = 1024
BATCH = 1
SEQ = 1024
DEPTH = 2

CHUNK = 64
N_A = DEPTH // 2
N_B = DEPTH - N_A
HEAD_DIM = 64
H_A = D_MODEL // HEAD_DIM
D_ATT = H_A * HEAD_DIM
Q_BLOCK = 128
H_B = D_MODEL // HEAD_DIM
KV_B = 4
GROUP_B = H_B // KV_B
WINDOW = 128
N_WIN_CHUNKS = WINDOW // CHUNK
D_FF = 2816
CONV_W = 3
EPS = 1e-6
NEG = -1e30

kernel_name = "yoco_fox_swa_sink_convffn_adaln"

def _rmsnorm(x, g):
    xf = x.astype(jnp.float32)
    y = xf * lax.rsqrt(jnp.mean(xf * xf, axis=-1, keepdims=True) + EPS)
    return (y * g.astype(jnp.float32)).astype(x.dtype)

def _modulate(x, g, shift, scale):
    return _rmsnorm(x, g) * (1.0 + scale[:, None, :]) + shift[:, None, :]

def _alibi_slopes(n_heads):
    return jnp.exp2(-8.0 * (jnp.arange(n_heads, dtype=jnp.float32) + 1.0) / n_heads)

def _forgetting_attention(h, w_in, b_f, w_o):
    B, S, _ = h.shape
    proj = h @ w_in
    q = proj[..., :D_ATT].reshape(B, S, H_A, HEAD_DIM)
    k = proj[..., D_ATT:2 * D_ATT].reshape(B, S, H_A, HEAD_DIM)
    v = proj[..., 2 * D_ATT:3 * D_ATT].reshape(B, S, H_A, HEAD_DIM)
    logf = jax.nn.log_sigmoid((proj[..., 3 * D_ATT:] + b_f).astype(jnp.float32))
    F = jnp.cumsum(logf, axis=1)
    F_k = F.transpose(0, 2, 1)
    nb = S // Q_BLOCK
    qb = q.reshape(B, nb, Q_BLOCK, H_A, HEAD_DIM).transpose(1, 0, 2, 3, 4)
    Fb = F.reshape(B, nb, Q_BLOCK, H_A).transpose(1, 0, 3, 2)
    kpos = jnp.arange(S)
    scale = 1.0 / math.sqrt(HEAD_DIM)

    def block(args):
        qi, Fi, i = args
        s = jnp.einsum('bqhd,bkhd->bhqk', qi, k).astype(jnp.float32) * scale
        s = s + Fi[..., None] - F_k[:, :, None, :]
        qpos = i * Q_BLOCK + jnp.arange(Q_BLOCK)
        s = jnp.where(kpos[None, :] <= qpos[:, None], s, NEG)
        p = jax.nn.softmax(s, axis=-1).astype(v.dtype)
        return jnp.einsum('bhqk,bkhd->bqhd', p, v)

    o = lax.map(block, (qb, Fb, jnp.arange(nb)))
    o = o.transpose(1, 0, 2, 3, 4).reshape(B, S, D_ATT)
    return o @ w_o

def _band(t):
    B, S, G, Dh = t.shape
    nc = S // CHUNK
    prev = jnp.pad(t[:, :S - CHUNK], ((0, 0), (CHUNK, 0), (0, 0), (0, 0)))
    cur = t.reshape(B, nc, CHUNK, G, Dh)
    prev = prev.reshape(B, nc, CHUNK, G, Dh)
    return jnp.concatenate([prev, cur], axis=2)

def _shared_kv(x, c_act, g, ada_w, ada_b, w_kv):
    B, S, _ = x.shape
    mod = c_act @ ada_w + ada_b
    shift, scale = jnp.split(mod, 2, axis=-1)
    h = _modulate(x, g, shift, scale)
    kv = h @ w_kv
    k = kv[..., :KV_B * HEAD_DIM].reshape(B, S, KV_B, HEAD_DIM)
    v = kv[..., KV_B * HEAD_DIM:].reshape(B, S, KV_B, HEAD_DIM)
    return _band(k), _band(v)

def _swa_sinks(h, w_q, sinks, w_o, k_band, v_band):
    B, S, _ = h.shape
    nc = S // CHUNK
    q = (h @ w_q).reshape(B, nc, CHUNK, KV_B, GROUP_B, HEAD_DIM)
    s = jnp.einsum('bnqgrd,bnkgd->bngrqk', q, k_band).astype(jnp.float32) / math.sqrt(HEAD_DIM)
    qi = jnp.arange(CHUNK)
    kj = jnp.arange(N_WIN_CHUNKS * CHUNK)
    dist = jnp.abs(qi[:, None] + CHUNK - kj[None, :]).astype(jnp.float32)
    slopes = _alibi_slopes(H_B).reshape(KV_B, GROUP_B)
    s = s - slopes[None, None, :, :, None, None] * dist[None, None, None, None]
    valid = (jnp.arange(nc)[:, None] > 0) | (kj[None, :] >= CHUNK)
    s = jnp.where(valid[None, :, None, None, None, :], s, NEG)
    sink = sinks.astype(jnp.float32).reshape(KV_B, GROUP_B)[None, None, :, :, None, None]
    m = jnp.maximum(jnp.max(s, axis=-1, keepdims=True), sink)
    e = jnp.exp(s - m)
    denom = jnp.sum(e, axis=-1, keepdims=True) + jnp.exp(sink - m)
    p = (e / denom).astype(v_band.dtype)
    o = jnp.einsum('bngrqk,bnkgd->bnqgrd', p, v_band).reshape(B, S, H_B * HEAD_DIM)
    return o @ w_o

def _conv_ffn(h, w_up, conv_w, conv_b, w_down):
    S = h.shape[1]
    u = h @ w_up
    up = jnp.pad(u, ((0, 0), (CONV_W - 1, 0), (0, 0)))
    conv = conv_b + sum(conv_w[j] * up[:, j:j + S] for j in range(CONV_W))
    gate, val = jnp.split(conv, 2, axis=-1)
    return (jax.nn.silu(gate) * val) @ w_down

def setup_inputs(seed: int = 0) -> dict:
    key = jax.random.key(seed)
    ks = jax.random.split(key, 24)
    D = D_MODEL
    nrm = jax.random.normal
    f32 = jnp.float32
    return {
        "x": nrm(ks[0], (BATCH, SEQ, D), f32),
        "c": nrm(ks[1], (BATCH, D), f32),
        "ada_w": nrm(ks[2], (DEPTH, D, 6 * D), f32) * (0.5 * D ** -0.5),
        "ada_b": nrm(ks[3], (DEPTH, 6 * D), f32) * 0.02,
        "norm1_g": 1.0 + 0.02 * nrm(ks[4], (DEPTH, D), f32),
        "norm2_g": 1.0 + 0.02 * nrm(ks[5], (DEPTH, D), f32),
        "a_w_in": nrm(ks[6], (N_A, D, 3 * D_ATT + H_A), f32) * D ** -0.5,
        "a_b_f": 2.0 + 0.5 * nrm(ks[7], (N_A, H_A), f32),
        "a_w_o": nrm(ks[8], (N_A, D_ATT, D), f32) * D_ATT ** -0.5,
        "kv_ada_w": nrm(ks[9], (D, 2 * D), f32) * (0.5 * D ** -0.5),
        "kv_ada_b": nrm(ks[10], (2 * D,), f32) * 0.02,
        "kv_norm_g": 1.0 + 0.02 * nrm(ks[11], (D,), f32),
        "kv_w": nrm(ks[12], (D, 2 * KV_B * HEAD_DIM), f32) * D ** -0.5,
        "b_w_q": nrm(ks[13], (N_B, D, H_B * HEAD_DIM), f32) * D ** -0.5,
        "b_sinks": nrm(ks[14], (N_B, H_B), f32),
        "b_w_o": nrm(ks[15], (N_B, H_B * HEAD_DIM, D), f32) * (H_B * HEAD_DIM) ** -0.5,
        "ffn_w_up": nrm(ks[16], (DEPTH, D, 2 * D_FF), f32) * D ** -0.5,
        "ffn_conv_w": nrm(ks[17], (DEPTH, CONV_W, 2 * D_FF), f32) * CONV_W ** -0.5,
        "ffn_conv_b": nrm(ks[18], (DEPTH, 2 * D_FF), f32) * 0.02,
        "ffn_w_down": nrm(ks[19], (DEPTH, D_FF, D), f32) * D_FF ** -0.5,
        "final_g": 1.0 + 0.02 * nrm(ks[20], (D,), f32),
    }

def reference(x, c, ada_w, ada_b, norm1_g, norm2_g, a_w_in, a_b_f, a_w_o,
              kv_ada_w, kv_ada_b, kv_norm_g, kv_w, b_w_q, b_sinks, b_w_o,
              ffn_w_up, ffn_conv_w, ffn_conv_b, ffn_w_down, final_g):
    c_act = jax.nn.silu(c)
    k_band = v_band = None
    for l in range(DEPTH):
        mod = c_act @ ada_w[l] + ada_b[l]
        sh1, sc1, g1, sh2, sc2, g2 = jnp.split(mod, 6, axis=-1)
        if l == N_A:
            k_band, v_band = _shared_kv(x, c_act, kv_norm_g, kv_ada_w, kv_ada_b, kv_w)
        h = _modulate(x, norm1_g[l], sh1, sc1)
        if l < N_A:
            y = _forgetting_attention(h, a_w_in[l], a_b_f[l], a_w_o[l])
        else:
            j = l - N_A
            y = _swa_sinks(h, b_w_q[j], b_sinks[j], b_w_o[j], k_band, v_band)
        x = x + g1[:, None, :] * y
        h = _modulate(x, norm2_g[l], sh2, sc2)
        x = x + g2[:, None, :] * _conv_ffn(h, ffn_w_up[l], ffn_conv_w[l], ffn_conv_b[l], ffn_w_down[l])
    return _rmsnorm(x, final_g)


_drawn_inputs = setup_inputs


def setup_inputs(seed=0):
    import zlib

    import numpy as np

    out = dict(_drawn_inputs(seed))
    spreads = {}
    factors = {'norm1_g': 8.0,
     'norm2_g': 6.618,
     'kv_ada_b': 8.0,
     'kv_norm_g': 8.0,
     'b_sinks': 4.38,
     'ffn_conv_b': 7.198,
     'final_g': 2.937}
    for name, (base, spread) in spreads.items():
        noise = np.random.default_rng([zlib.crc32(name.encode()), seed]).standard_normal(out[name].shape)
        drawn = base * np.exp(spread * noise) if base else spread * noise
        out[name] = __import__('jax').numpy.asarray(drawn.astype(out[name].dtype))
    for name, factor in factors.items():
        out[name] = (out[name] * factor).astype(out[name].dtype)
    return out
```

```python
from contextlib import ExitStack

import numpy as np

import concourse.bass as bass
from concourse import mybir

F32 = mybir.dt.float32
F32R = mybir.dt.float32r
ALU = mybir.AluOpType
ACT = mybir.ActivationFunctionType

P = 128
D = 1024
S = 1024
HALF = 512
KT = D // P
HD = 64
NH = D // HD
KV = 4
CH = 64
FF = 2816
FT = FF // P
NG = 4
EPS = 1e-6
NEG = -1e30
QSCALE = 1.0 / 8.0

W_ATT_A = 0
W_OUT_A = W_ATT_A + 6 * NG
W_FFN = [W_OUT_A + 8, 0]
W_KV = W_FFN[0] + 3 * FT
W_Q_B = W_KV + 4
W_OUT_B = W_Q_B + 8
W_FFN[1] = W_OUT_B + 8
W_TILES = W_FFN[1] + 3 * FT
RAW = 2
SPL = 3

M_SH1, M_SC1, M_G1, M_SH2, M_SC2, M_G2 = (8 * i for i in range(6))
M_L1 = 48
M_KV = 96
G_N1, G_N2, G_KV, G_FIN = 0, 16, 32, 40


def tasks_before(i):
    return i if i <= 4 else 2 * i - 4


def tasks_to(t):
    return 12 * (t // 8) + tasks_before(t % 8)


def program(nc, x_t, c_t, ada_w, kv_ada_w, mod_b, gains, w_stream, w_f, b_f, sinks, conv, ident, mask,
            stair, alibi, out_t):
    ctx = ExitStack()
    with ctx:
        base = (nc.sbuf_base + 63) // 64 * 64
        K_ = 1024

        def at(name, shape, dt, kb):
            return nc.alloc_sbuf_tensor_at(name, shape, dt, offset=base + int(kb * K_))

        def sem(name):
            return ctx.enter_context(nc.semaphore(name))

        H = at("H", [P, KT, 2, S], F32R, 0)
        ada_raw0 = at("ada_raw0", [P, 4, KT, 512], F32, 0)
        X = at("X", [P, KT, S], F32, 64)
        w_raw = at("w_raw", [P, RAW, 1024], F32, 96)
        w_spl = at("w_spl", [P, SPL, 2, 1024], F32R, 104)
        QS = [at("QS0", [P, 2, S], F32R, 64), at("QS1", [P, 2, S], F32R, 128)]
        KS = [at("KS0", [P, 2, S], F32R, 72), at("KS1", [P, 2, S], F32R, 136)]
        KL = [at("KL0", [P, 2, S], F32R, 80), at("KL1", [P, 2, S], F32R, 144)]
        negF = at("negF", [P, 2, S], F32, 88)
        V = at("V", [P, 8, 4, 2, HD], F32R, 152)
        Pm = at("Pm", [P, 2, S], F32, 168)
        ada_acc_a = at("ada_acc_a", [P, 2, 512], F32, 168)
        O_raw = at("O_raw", [P, 4, S], F32, 168)
        PT = at("PT", [P, 2, 8, 256], F32R, 176)
        ada_raw_a = at("ada_raw_a", [P, KT, 512], F32, 176)
        O_st = at("O_st", [P, S], F32, 192)
        O_tmp = at("O_tmp", [P, 256], F32, 196)
        zb = at("zb", [P, 8, 16], F32, 128)
        za = at("za", [P, 8, 16], F32, 128.5)
        ze = at("ze", [P, 8, 16], F32, 129)
        zl = at("zl", [P, 8, 16], F32, 129.5)
        lf = at("lf", [P, 8, 16], F32, 130)
        wf_raw = at("wf_raw", [P, KT, 16], F32, 130.5)
        wf = at("wf", [P, 2, KT, 16], F32R, 131)
        stair_s = at("stair_s", [P, S], F32, 132)
        nF16 = at("nF16", [16, S], F32, 136)
        mask_f = at("mask_f", [P, P], F32, 140)
        sq = at("sq", [P, 2, S], F32, 144)
        ss = at("ss", [P, S], F32, 152)
        rt = at("rt", [P, S], F32, 156)
        ada_acc0 = at("ada_acc0", [P, 4, 512], F32, 128)
        rstd = at("rstd", [P, S], F32, 180)
        tn = at("tn", [P, 2, S], F32, 184)
        hf = at("hf", [P, 2, S], F32, 192)
        hid = at("hid", [P, 2, 2, S], F32R, 128)
        cG = at("cG", [P, 2, S], F32, 144)
        cV = at("cV", [P, 2, S], F32, 152)
        ada_raw_f = at("ada_raw_f", [P, KT, 1024], F32, 160)
        ada_acc_f = at("ada_acc_f", [P, 1024], F32, 192)
        PAD = CH
        KSB = at("KSB", [P, KV, PAD + S], F32R, 128)
        KLB = at("KLB", [P, KV, PAD + S], F32R, 145)
        VB = at("VB", [P, 8, KV, 2, HD], F32R, 162)
        VBs = at("VBs", [P, 8, KV, 2, HD], F32R, 64)
        QB = at("QB", [P, 2, S // CH, 2, CH], F32R, 80)
        PB = at("PB", [P, 2, 4, P], F32, 178)
        PTB = at("PTB", [P, 2, 512], F32R, 182)
        bias_s = at("bias_s", [P, 8, P], F32, 186)
        O_stB = at("O_stB", [P, S], F32, 190)
        O_tmpB = at("O_tmpB", [P, 4, CH], F32, 194)
        id_f = at("id_f", [P, P], F32, 200)
        id_r = at("id_r", [P, P], F32R, 200.5)
        mask_r = at("mask_r", [P, P], F32R, 201)
        ones = at("ones", [P, P], F32, 201.5)
        mods = at("mods", [P, 112], F32, 202)
        modb = at("modb", [P, 112], F32, 202.5)
        gain = at("gain", [P, 48], F32, 203)
        coef = at("coef", [P, 48], F32, 203.25)
        conv_s = at("conv_s", [P, 2, 2 * FT, 4], F32, 203.5)
        bf_s = at("bf_s", [P, 16], F32, 205)
        sink_s = at("sink_s", [P, 8], F32, 205.125)
        c_s = at("c_s", [P, KT], F32, 205.1875)
        c_act = at("c_act", [P, KT], F32, 205.25)
        eps_s = at("eps_s", [P, 1], F32, 205.3125)
        one_s = at("one_s", [P, 1], F32, 205.375)
        pace = at("pace", [P, 2], F32, 206)
        mx = at("mx", [P, 2], F32, 205.4375)
        nmx = at("nmx", [P, 2], F32, 205.5)
        den = at("den", [P, 2], F32, 205.5625)
        rden = at("rden", [P, 2], F32, 205.625)
        mxB = at("mxB", [P, 2, 4], F32, 205.6875)
        nmB = at("nmB", [P, 2, 4], F32, 205.75)
        dnB = at("dnB", [P, 2, 4], F32, 205.8125)
        esB = at("esB", [P, 2, 4], F32, 205.875)
        rdB = at("rdB", [P, 2, 4], F32, 205.9375)

        BK = [ctx.enter_context(nc.psum_tensor(f"bank{i}", [P, 4, HALF], F32)) for i in range(2)]

        def bank(i, lo=0, hi=HALF):
            return BK[i // 4][:, i % 4, lo:hi]

        def pair(i):
            return BK[i // 4][:, i % 4:i % 4 + 2, :].rearrange("p a b -> p (a b)")

        T_BANK, PV_BANK, PJ_BANK = 4, 6, 7

        dO = nc.dram_tensor("scratch_o", [8, P, S], F32).ap()
        dX = nc.dram_tensor("scratch_x", [KT, P, S], F32).ap()
        dF = nc.dram_tensor("scratch_f", [16, S], F32).ap()

        raw_in = [sem(f"raw_in{i}") for i in range(RAW)]
        w_hi = sem("w_hi")
        w_ready = sem("w_ready")
        w_used = sem("w_used")
        const_in = sem("const_in")
        gate_in = sem("gate_in")
        cact_done = sem("cact_done")
        set_done = sem("set_done")
        ada0_in = [sem(f"ada0_in{i}") for i in range(4)]
        ada_in = sem("ada_in")
        ada_step = sem("ada_step")
        ada_ps = sem("ada_ps")
        ada_ev = sem("ada_ev")
        x_in = [sem(f"x_in{i}") for i in range(4)]
        sq_done = sem("sq_done")
        ss_done = sem("ss_done")
        ms_ps = sem("ms_ps")
        rt_done = sem("rt_done")
        rs_done = sem("rs_done")
        t_done = sem("t_done")
        h_hi = sem("h_hi")
        h_lo = sem("h_lo")
        z_ps = sem("z_ps")
        z_v = sem("z_v")
        z_a = sem("z_a")
        f_ps = sem("f_ps")
        f_out = sem("f_out")
        const_r = sem("const_r")
        nf_in = [sem(f"nf_in{i}") for i in range(2)]
        qk_ps = sem("qk_ps")
        qk_hi = sem("qk_hi")
        qk_lo = sem("qk_lo")
        v_ps = sem("v_ps")
        v_hi = sem("v_hi")
        v_lo = sem("v_lo")
        s_ps = sem("s_ps")
        s_read = sem("s_read")
        s_max = sem("s_max")
        exp_done = sem("exp_done")
        rd_done = sem("rd_done")
        p_norm = sem("p_norm")
        t_ps = sem("t_ps")
        pt_hi = sem("pt_hi")
        pt_lo = sem("pt_lo")
        pv_ps = sem("pv_ps")
        o_tmp = sem("o_tmp")
        o_add = sem("o_add")
        o_out = [sem(f"o_out{i}") for i in range(2)]
        o_in = [sem(f"o_in{i}") for i in range(4)]
        o_hi = sem("o_hi")
        o_lo = sem("o_lo")
        wo_ps = sem("wo_ps")
        wo_ev = sem("wo_ev")
        up_ps = sem("up_ps")
        cv0 = sem("cv0")
        cv1 = sem("cv1")
        cv2 = sem("cv2")
        silu_done = sem("silu_done")
        prod = sem("prod")
        hid_hi = sem("hid_hi")
        hid_lo = sem("hid_lo")
        dn_ps = sem("dn_ps")
        dn_ev = sem("dn_ev")
        x_out = sem("x_out")
        kb_ps = sem("kb_ps")
        kb_hi = sem("kb_hi")
        kb_lo = sem("kb_lo")
        vs_in = sem("vs_in")
        sB_ps = sem("sB_ps")
        sB_read = sem("sB_read")
        mB = sem("mB")
        expB = sem("expB")
        dB = sem("dB")
        pB = sem("pB")
        tB_ps = sem("tB_ps")
        ptB_hi = sem("ptB_hi")
        ptB_lo = sem("ptB_lo")
        pvB_ps = sem("pvB_ps")
        o_tmpB = sem("o_tmpB_s")
        o_addB = sem("o_addB")
        qB_ps = sem("qB_ps")
        qB_hi = sem("qB_hi")
        qB_lo = sem("qB_lo")
        y_done = sem("y_done")
        y_out = [sem(f"y_out{i}") for i in range(2)]

        N_ADA_A = 4 + 2 * NG
        NORM_IN = [None, (wo_ev, 0), (dn_ev, 80), (wo_ev, 8), (dn_ev, 88 + 80)]
        MODS = [(G_N1, M_SC1, M_SH1), (G_N2, M_SC2, M_SH2), (G_KV, M_KV + 8, M_KV),
                (G_N1 + 8, M_L1 + M_SC1, M_L1 + M_SH1), (G_N2 + 8, M_L1 + M_SC2, M_L1 + M_SH2)]

        block = ctx.enter_context(nc.Block())

        @block.sync
        def _(sp):
            n_const = 0
            for dst, src in ((c_s, c_t), (modb, mod_b), (gain, gains), (bf_s, b_f), (sink_s, sinks),
                             (id_f, ident), (conv_s, conv)):
                sp.dma_start(dst[:], src).then_inc(const_in, 16)
            for j in range(4):
                sp.dma_start(ada_raw0[:, j], ada_w[0].rearrange("(k p) n -> p k n", p=P)[
                    :, :, 512 * j:512 * j + 512]).then_inc(ada0_in[j], 16)
                sp.dma_start(X[:, 2 * j:2 * j + 2], x_t.rearrange("k p s -> p k s")[
                    :, 2 * j:2 * j + 2]).then_inc(x_in[j], 16)

            def load(pos, u, free):
                if free is not None:
                    sp.wait_ge(w_ready, free)
                sp.dma_start(w_raw[:, u % RAW, :], w_stream[pos]).then_inc(raw_in[u % RAW], 16)

            for u in range(6):
                load(u, u, u - 1 if u >= RAW else None)
            with sp.Fori(1, W_TILES // 6) as it:
                for u in range(6):
                    load(it * 6 + u, u, it * 6 + u - 1)
            for pos in range(W_TILES // 6 * 6, W_TILES):
                load(pos, pos, pos - 1)

        @block.gpsimd
        def _(pool):
            def split(pos, u, raw_value, free):
                pool.wait_ge(raw_in[u % RAW], raw_value)
                if free is not None:
                    pool.wait_ge(w_used, free)
                pool.tensor_tensor(pace[:, 0:1], one_s[:], one_s[:], ALU.mult)
                hi, lo = w_spl[:, u % SPL, 0, :], w_spl[:, u % SPL, 1, :]
                pool.tensor_scalar(hi, w_raw[:, u % RAW, :], 1.0, 1.0, ALU.mult, ALU.mult).then_inc(w_hi, 1)
                pool.wait_ge(w_hi, pos + 1)
                pool.tensor_tensor(lo, w_raw[:, u % RAW, :], hi.bitcast(F32), ALU.subtract).then_inc(w_ready, 1)

            pool.wait_ge(set_done, 1)
            for u in range(6):
                split(u, u, 16 * (u // RAW + 1), u - SPL + 1 if u >= SPL else None)
            with pool.Fori(1, W_TILES // 6) as it:
                for u in range(6):
                    split(it * 6 + u, u, it * 48 + 16 * (u // RAW + 1), it * 6 + (u - SPL + 1))
            for pos in range(W_TILES // 6 * 6, W_TILES):
                split(pos, pos, 16 * (pos // RAW + 1), pos - SPL + 1)

        @block.tensor
        def _(pe):
            def product(dst, stat, mov, ks=range(KT), release=0):
                for k in ks:
                    for a, b in ((0, 0), (0, 1), (1, 0)):
                        last = pe.matmul(dst, stat(k, a), mov(k, b), start=(k == 0 and a + b == 0),
                                         stop=(k == KT - 1 and a == 1))
                        if release:
                            last.then_inc(w_used, release)
                            release = 0
                return last

            def h_cols(lo, n):
                return lambda k, part: H[:, k, part, lo:lo + n]

            def w_tile(u):
                return lambda k, part: w_spl[:, u % SPL, part, k * P:k * P + P]

            def ada_cols(acc, cols, need, slot_bank, col0):
                pe.wait_ge(ada_step, need)
                for j in range(cols):
                    last = pe.matmul(bank(slot_bank, col0 + j, col0 + j + 1), acc[:, j * P:j * P + P],
                                     one_s[:], start=True, stop=True)
                last.then_inc(ada_ps, 1)

            def mean_squares(n, release=0):
                pe.wait_ge(ss_done, 8 * n + 8)
                for hh in range(2):
                    last = pe.matmul(bank(hh), ones[:], ss[:, hh * HALF:hh * HALF + HALF], start=True, stop=True)
                    if hh == 0 and release:
                        last.then_inc(w_used, release)
                last.then_inc(ms_ps, 1)

            pe.wait_ge(set_done, 1)
            for j in range(4):
                if j:
                    pe.wait_ge(ada_ev, j)
                ada_cols(ada_acc0[:, j], 4, 8 * (j + 1), PV_BANK, 0)
            mean_squares(0)
            pe.wait_ge(h_lo, 8)
            pe.wait_ge(z_v, 1)
            for tt in range(8):
                for k in range(KT):
                    for a, b in ((0, 0), (0, 1), (1, 0)):
                        last = pe.matmul(bank(2, tt * 16, tt * 16 + 16), H[:, k, b, tt * P:tt * P + P],
                                         wf[:, a, k, :], start=(k == 0 and a + b == 0),
                                         stop=(k == KT - 1 and a == 1))
            last.then_inc(z_ps, 1)
            pe.wait_ge(z_v, 5)
            for hh in range(2):
                for t in range(4 * hh + 4):
                    lo = max(t * P, hh * HALF)
                    last = pe.matmul(bank(hh, lo - hh * HALF, HALF)[0:16], lf[:, t, :],
                                     stair_s[:, lo - t * P:(hh + 1) * HALF - t * P], start=(t == 0),
                                     stop=(t == 4 * hh + 3))
            last.then_inc(f_ps, 1)
            pe.wait_ge(z_v, 6)

            with pe.Fori(0, NG) as g:
                for n in range(4):
                    u = n // 2
                    if n % 2 == 0:
                        pe.wait_ge(w_ready, g * 6 + (u + 1))
                    last = product(bank(n), w_tile(u), h_cols((n % 2) * HALF, HALF), release=int(n == 2))
                    last.then_inc(qk_ps, 1)
                pe.wait_ge(w_ready, g * 6 + 4)
                for tt in range(8):
                    if tt < 4:
                        pe.wait_ge(qk_lo, g * 8 + (tt + 1))
                    else:
                        pe.wait_ge(v_lo, g * 8 + (tt - 3))
                    last = product(bank(tt % 4, 0, 256), lambda k, a: H[:, k, a, tt * P:tt * P + P],
                                   lambda k, b: w_spl[:, 2 - k // 4 * 2, b, (k % 4) * 256:(k % 4) * 256 + 256],
                                   release=int(tt == 0))
                    last.then_inc(v_ps, 1)
                for j in range(2):
                    ada_cols(ada_acc_a[:, j], 4, g * 16 + (32 + 8 * (j + 1)), PV_BANK, 4 * j)
                pe.wait_ge(v_lo, g * 8 + 8)
                pe.wait_ge(ada_ev, g * 2 + 6)

                def scores(t):
                    pp, e, i = t // 16, t // 8 % 2, t % 8
                    if t % 16 == 0:
                        pe.wait_ge(qk_lo, g * 8 + (4 + 4 * pp))
                    if t >= 2:
                        pe.wait_ge(s_read, g * 32 + (t - 1))
                    n = (i + 1) * P
                    for c0 in range(0, n, HALF):
                        m = min(HALF, n - c0)
                        dst = bank(2 * (t % 2) + c0 // HALF, 0, m)
                        q = QS[pp][:, e, i * P:i * P + P]
                        first = pe.matmul(dst, q, KS[pp][:, e, c0:c0 + m], start=True, stop=False)
                        if t == 16:
                            first.then_inc(w_used, 1)
                        last = pe.matmul(dst, q, KL[pp][:, e, c0:c0 + m], start=False, stop=True)
                        if c0 + m == n:
                            last = pe.matmul(bank(2 * (t % 2) + c0 // HALF, m - P, m), id_r[:], mask_r[:],
                                             start=False, stop=True, skip_group_check=True)
                    last.then_inc(s_ps, 1)

                def turn(t):
                    pe.wait_ge(p_norm, g * 32 + (t + 1))
                    i = t % 8
                    for j in range(1 if i < 4 else 2):
                        before = tasks_to(t - 1) + j if t and (j == 0 or i > 4) else None
                        if j == 1 and i == 4 and t > 4:
                            before = tasks_to(t - 5) + 1
                        if before is not None:
                            pe.wait_ge(pt_lo, g * 48 + (before + 1))
                        kbs = range(4 * j, min(4 * j + 4, i + 1))
                        for kb in kbs:
                            last = pe.transpose(bank(T_BANK + j, (kb % 4) * P, (kb % 4) * P + P),
                                                Pm[:, t % 2, kb * P:kb * P + P], id_f[:])
                        last.then_inc(t_ps, 1)

                def values(q):
                    hl, c = q // 4, q % 4
                    pe.wait_ge(pt_lo, g * 48 + tasks_to(2 * q + 2))
                    if q:
                        pe.wait_ge(o_add, g * 16 + q)
                    for kb in range(2 * c + 2):
                        lo = 0 if kb <= 2 * c else P
                        for part in range(2):
                            last = pe.matmul(bank(PV_BANK, lo, 256), V[:, kb, hl, :, :].rearrange("p a b -> p (a b)"),
                                             PT[:, part, kb, lo:256], start=(kb == 0 and part == 0),
                                             stop=(kb == 2 * c + 1 and part == 1), skip_group_check=True)
                    last.then_inc(pv_ps, 1)

                def next_qk(t):
                    n = 4 + t // 4
                    u = 4 + (n - 4) // 2
                    if t % 8 == 0:
                        pe.wait_ge(w_ready, g * 6 + (u + 1))
                    if t % 4 == 0 and n > 4:
                        pe.wait_ge(qk_lo, g * 8 + n)
                    ks = range(2 * (t % 4), 2 * (t % 4) + 2)
                    last = product(bank(PJ_BANK), w_tile(u), h_cols((n % 2) * HALF, HALF), ks,
                                   release={0: 2, 8: 1}.get(t, 0))
                    if t % 4 == 3:
                        last.then_inc(qk_ps, 1)

                for t in range(34):
                    if t < 32:
                        scores(t)
                    if t % 2 and t >= 3:
                        values((t - 3) // 2)
                    if t < 16:
                        next_qk(t)
                    if 1 <= t <= 32:
                        turn(t - 1)

            def out_proj(layer):
                w0 = [W_OUT_A, W_OUT_B][layer]
                for m in range(8):
                    pe.wait_ge(w_ready, w0 + m + 1)
                    if m >= 2:
                        pe.wait_ge(wo_ev, 8 * layer + m - 1)
                    for k in range(KT):
                        if m == 0:
                            pe.wait_ge(o_lo, 8 * layer + k + 1)
                        for hh in range(2):
                            last = product(bank(4 + 2 * (m % 2) + hh), w_tile(w0 + m), h_cols(hh * HALF, HALF), [k],
                                           release=int(k == 0 and hh == 0 and (m > 0 or layer == 1)))
                    last.then_inc(wo_ps, 1)

            def ffn(layer):
                w0 = W_FFN[layer]
                u0 = 2 * FT * layer

                def up_tile(slot, gv, pos, before, wait_bank=True, first=False, release=1):
                    pe.wait_ge(w_ready, pos + 1)
                    if wait_bank:
                        pe.wait_ge(cv2, before - 1)
                    for k in range(KT):
                        if first:
                            pe.wait_ge(h_lo, 8 * [1, 4][layer] + k + 1)
                        for hh in range(2):
                            last = product(bank(2 * gv + hh), w_tile(slot), h_cols(hh * HALF, HALF), [k],
                                           release=release if k == 0 and hh == 0 else 0)
                    last.then_inc(up_ps, 1)

                def down(slot, pos, hid_need, ev_need, ada_need):
                    pe.wait_ge(w_ready, pos + 2)
                    pe.wait_ge(hid_lo, hid_need)
                    if ada_need is not None:
                        pe.wait_ge(ada_ev, ada_need)
                    for m in range(8):
                        if m >= 2 or ev_need is not None:
                            pe.wait_ge(dn_ev, (ev_need if ev_need is not None else 88 * layer) + m - 1)
                        for hh in range(2):
                            for s in range(2):
                                for a, b in ((0, 0), (0, 1), (1, 0)):
                                    last = pe.matmul(bank(4 + 2 * (m % 2) + hh),
                                                     w_spl[:, (slot + s) % SPL, a, m * P:m * P + P],
                                                     hid[:, s, b, hh * HALF:hh * HALF + HALF],
                                                     start=(s == 0 and a + b == 0), stop=(s == 1 and a == 1))
                                    if m + hh + s + a + b == 0:
                                        last.then_inc(w_used, 1)
                        last.then_inc(dn_ps, 1)

                up_tile(w0, 0, w0, u0, False, True, 0)
                up_tile(w0 + 1, 1, w0 + 1, u0 + 1, False)
                up_tile(w0 + 2, 0, w0 + 2, u0 + 2)
                up_tile(w0 + 3, 1, w0 + 3, u0 + 3)

                def body(it, ada, ada_before):
                    pos = it * 6 + (w0 - 2)
                    ut = it * 4 + u0
                    up_tile(w0 - 2, 0, pos, ut)
                    up_tile(w0 - 1, 1, pos + 1, ut + 1)
                    down(w0, pos + 2, it * 2 + 22 * layer, it * 8 + (88 * layer - 8),
                         None if ada_before is None else ada_before)
                    up_tile(w0 + 2, 0, pos + 4, ut + 2, release=2)
                    up_tile(w0 + 3, 1, pos + 5, ut + 3)
                    if ada:
                        pe.wait_ge(dn_ev, it * 8 + (88 * layer - 8) + 7)
                        ada_cols(ada_acc_f, 8, it * 8 + 96, 4, 0)

                def body1():
                    pos = w0 + 4
                    up_tile(w0 + 4, 0, pos, u0 + 4)
                    up_tile(w0 + 5, 1, pos + 1, u0 + 5)
                    down(w0, pos + 2, 22 * layer + 2, None, None)
                    up_tile(w0 + 2, 0, pos + 4, u0 + 6, release=2)
                    up_tile(w0 + 3, 1, pos + 5, u0 + 7)
                    if layer == 0:
                        pe.wait_ge(dn_ev, 7)
                        ada_cols(ada_acc_f, 8, 104, 4, 0)

                body1()
                if layer == 0:
                    with pe.Fori(2, 9) as it:
                        body(it, True, it + (N_ADA_A - 1))
                    with pe.Fori(9, 11) as it:
                        body(it, False, N_ADA_A + 8)
                else:
                    with pe.Fori(2, 11) as it:
                        body(it, False, None)
                down(w0 + 64, w0 + 64, 22 * (layer + 1), 88 * layer + 80, None)

            out_proj(0)
            mean_squares(1, 1)
            ffn(0)
            mean_squares(2, 2)

            for n in range(4):
                if n % 2 == 0:
                    pe.wait_ge(w_ready, W_KV + n // 2 + 1)
                if n == 0:
                    pe.wait_ge(h_lo, 24)
                last = product(bank(n), w_tile(W_KV + n // 2), h_cols((n % 2) * HALF, HALF), release=int(n == 2))
                last.then_inc(kb_ps, 1)
            pe.wait_ge(w_ready, W_KV + 4)
            for tt in range(8):
                if tt >= 4:
                    pe.wait_ge(kb_lo, tt + 1)
                last = product(bank(4 + tt % 4, 0, 256), lambda k, a: H[:, k, a, tt * P:tt * P + P],
                               lambda k, b: w_spl[:, (W_KV + 2 + k // 4) % SPL, b, (k % 4) * 256:(k % 4) * 256 + 256],
                               release=int(tt == 0))
                last.then_inc(kb_ps, 1)

            def q_quarter(hp, qd):
                if qd == 0:
                    pe.wait_ge(w_ready, W_Q_B + hp + 1)
                if qd % 2 == 0 and 2 * hp + qd // 2 >= 2:
                    pe.wait_ge(qB_lo, 2 * hp + qd // 2 - 1)
                ks = range(4 * (qd % 2), 4 * (qd % 2) + 4)
                last = product(bank(6 + qd // 2), w_tile(W_Q_B + hp), h_cols(qd // 2 * HALF, HALF), ks,
                               release=(1 if hp else 2) if qd == 0 else 0)
                if qd % 2:
                    last.then_inc(qB_ps, 1)

            def scores_b(u):
                hp, qd = u // 4, u % 4
                if qd == 0:
                    pe.wait_ge(qB_lo, 2 * hp + 2)
                if u >= 2:
                    pe.wait_ge(sB_read, u - 1)
                for j in range(4):
                    n = 4 * qd + j
                    q = QB[:, hp % 2, n, :, :].rearrange("p e q -> p (e q)")
                    pe.matmul(bank(u % 2, j * P, j * P + P), q, KSB[:, hp // 2, n * CH:n * CH + P],
                              start=True, stop=False)
                    last = pe.matmul(bank(u % 2, j * P, j * P + P), q, KLB[:, hp // 2, n * CH:n * CH + P],
                                     start=False, stop=True)
                last.then_inc(sB_ps, 1)

            def turn_b(u):
                pe.wait_ge(pB, u + 1)
                if u >= 2:
                    pe.wait_ge(ptB_lo, u - 1)
                for j in range(4):
                    last = pe.transpose(bank(2 + u % 2, j * P, j * P + P), PB[:, u % 2, j, :], id_f[:])
                last.then_inc(tB_ps, 1)

            def values_b(u):
                hp, qd = u // 4, u % 4
                g = hp // 2
                pe.wait_ge(ptB_lo, u + 1)
                if u >= 2:
                    pe.wait_ge(o_addB, 2 * (u - 1))
                for j in range(4):
                    n = 4 * qd + j
                    v = (VB if n % 2 else VBs)[:, n // 2, g, :, :].rearrange("p a b -> p (a b)")
                    for part in range(2):
                        last = pe.matmul(bank(4 + u % 2, j * P, j * P + P), v, PTB[:, part, j * P:j * P + P],
                                         start=(part == 0), stop=(part == 1))
                last.then_inc(pvB_ps, 1)

            pe.wait_ge(h_lo, 32)
            pe.wait_ge(kb_lo, 12)
            for qd in range(4):
                q_quarter(0, qd)
            for u in range(34):
                if u < 32:
                    if u == 0:
                        pe.wait_ge(vs_in, 48)
                    scores_b(u)
                if u < 28:
                    q_quarter(u // 4 + 1, u % 4)
                if u >= 2:
                    values_b(u - 2)
                if 1 <= u <= 32:
                    turn_b(u - 1)
            out_proj(1)
            mean_squares(3, 1)
            ffn(1)
            mean_squares(4)

        @block.scalar
        def _(act):
            def squares(n):
                def one(k):
                    if n == 0:
                        act.wait_ge(x_in[k // 2], 16)
                    else:
                        s_, v_ = NORM_IN[n]
                        act.wait_ge(s_, v_ + k + 1)
                    if k >= 2:
                        act.wait_ge(ss_done, 8 * n + k - 1)
                    nc.scalar.activation(sq[:, k % 2], X[:, k], ACT.Square).then_inc(sq_done, 1)
                return one

            def root(n):
                act.wait_ge(ms_ps, n + 1)
                nc.scalar.activation(rt[:], pair(0), ACT.Sqrt, bias=eps_s[:]).then_inc(rt_done, 1)

            def modulate(hn):
                sh = MODS[hn][2]
                for k in range(KT):
                    act.wait_ge(t_done, 8 * hn + k + 1)
                    if k >= 2:
                        act.wait_ge(h_lo, 8 * hn + k - 1)
                    a, b = coef[:, 8 * hn + k:8 * hn + k + 1], mods[:, sh + k:sh + k + 1]
                    nc.scalar.activation(hf[:, k % 2], tn[:, k % 2], ACT.Identity, scale=a, bias=b)
                    nc.scalar.activation(H[:, k, 0], tn[:, k % 2], ACT.Identity, scale=a, bias=b).then_inc(h_hi, 1)

            act.wait_ge(const_in, 16 * 7)
            nc.scalar.activation(c_act[:], c_s[:], ACT.Silu).then_inc(cact_done, 1)
            act.wait_ge(set_done, 1)
            nc.scalar.activation(id_r[:], id_f[:], ACT.Copy)
            for k in range(8):
                squares(0)(k)
            root(0)
            modulate(0)
            act.wait_ge(h_lo, 8)
            act.dma_start(wf_raw[:], w_f).then_inc(gate_in, 16)
            act.dma_start(stair_s[:], stair).then_inc(gate_in, 16)
            act.dma_start(mask_f[:], mask).then_inc(gate_in, 16)
            act.wait_ge(gate_in, 48)
            nc.scalar.activation(mask_r[:], mask_f[:], ACT.Copy)
            nc.scalar.activation(wf[:, 0], wf_raw[:], ACT.Copy).then_inc(const_r, 1)
            act.wait_ge(z_v, 3)
            nc.scalar.activation(ze[:], za[:], ACT.Exp, scale=-1.0).then_inc(z_a, 1)
            act.wait_ge(z_a, 1)
            nc.scalar.activation(zl[:], ze[:], ACT.Ln, bias=one_s[:]).then_inc(z_a, 1)
            act.wait_ge(z_v, 6)
            act.dma_start(dF, nF16[:]).then_inc(f_out, 16)
            act.wait_ge(f_out, 16)

            with act.Fori(0, NG) as g:
                def load_negf(hl):
                    act.dma_start(negF[:, hl % 2, :], dF[bass.ds(g * 4 + hl, 1), :].partition_broadcast(P)[:, 0, :]
                                  ).then_inc(nf_in[hl % 2], 16)

                def load_ada(j):
                    act.dma_start(ada_raw_a[:], ada_w[0].rearrange("(k p) n -> p k n", p=P)[
                        :, :, bass.ds(g * 1024 + (2048 + 512 * j), 512)]).then_inc(ada_in, 16)

                def qk_high(n):
                    pp, is_k, hh = n // 4, n // 2 % 2, n % 2
                    act.wait_ge(qk_ps, g * 8 + (n + 1))
                    src = bank(n if n < 4 else PJ_BANK)
                    cols = slice(hh * HALF, hh * HALF + HALF)
                    for e in range(2):
                        rows = src[64 * e:64 * e + 64]
                        if is_k:
                            nc.scalar.activation(KS[pp][64:128, e, cols], rows, ACT.Copy)
                            last = nc.scalar.activation(KS[pp][0:64, e, cols], rows, ACT.Copy)
                        else:
                            last = nc.scalar.activation(QS[pp][0:64, e, cols], rows, ACT.Copy, scale=QSCALE)
                    last.then_inc(qk_hi, 1)

                load_ada(0)
                load_negf(0)
                load_negf(1)
                for n in range(4):
                    qk_high(n)
                    if n == 1:
                        act.wait_ge(ada_step, g * 16 + 40)
                        load_ada(1)
                for tt in range(8):
                    act.wait_ge(v_ps, g * 8 + (tt + 1))
                    nc.scalar.activation(V[:, tt, :, 0, :], bank(tt % 4, 0, 256).rearrange("p (h d) -> p h d", h=4),
                                         ACT.Copy).then_inc(v_hi, 1)
                for t in range(34):
                    if t < 32:
                        n = (t % 8 + 1) * P
                        act.wait_ge(s_max, g * 32 + (t + 1))
                        nc.scalar.activation(Pm[:, t % 2, 0:n], Pm[:, t % 2, 0:n], ACT.Exp,
                                             bias=nmx[:, t % 2:t % 2 + 1],
                                             accum_out=den[:, t % 2:t % 2 + 1]).then_inc(exp_done, 1)
                    if t % 2 and t >= 3:
                        q = (t - 3) // 2
                        e = q // 4 % 2
                        act.wait_ge(pv_ps, g * 16 + (q + 1))
                        if q:
                            act.wait_ge(o_add, g * 16 + q)
                        nc.scalar.activation(O_tmp[64 * e:64 * e + 64, :], bank(PV_BANK, 0, 256)[64 - 64 * e:128 - 64 * e],
                                             ACT.Copy).then_inc(o_tmp, 1)
                    if t < 16 and t % 4 == 3:
                        qk_high(4 + t // 4)
                    if 1 <= t <= 32:
                        tau = t - 1
                        i = tau % 8
                        for j in range(1 if i < 4 else 2):
                            act.wait_ge(t_ps, g * 48 + (tasks_to(tau) + j + 1))
                            if tau % 2 == 0 and tau >= 2 and j == 0:
                                act.wait_ge(pv_ps, g * 16 + tau // 2)
                            k0, k1 = 4 * j, min(4 * j + 4, i + 1)
                            nc.scalar.activation(
                                PT[:, 0, k0:k1, (tau % 2) * P:(tau % 2) * P + P],
                                bank(T_BANK + j, 0, (k1 - k0) * P).rearrange("p (k q) -> p k q", q=P),
                                ACT.Copy).then_inc(pt_hi, 1)
                    if t in (10, 18):
                        act.wait_ge(s_read, g * 32 + (t - 2))
                        load_negf(2 if t == 10 else 3)
                    if t % 8 == 2 and t > 2 or t == 33:
                        hl = 3 if t == 33 else (t - 3) // 8
                        act.wait_ge(o_add, g * 16 + 4 * (hl + 1))
                        e = hl % 2
                        act.dma_start(dO[bass.ds(g * 2 + hl // 2, 1), 64 * e:64 * e + 64, :],
                                      O_st[64 * e:64 * e + 64, :]).then_inc(o_out[e], 16)

            def out_proj(layer, x_src):
                raw = O_raw
                for j in range(4):
                    act.dma_start(X[:, 2 * j:2 * j + 2], x_src.rearrange("k p s -> p k s")[
                        :, 2 * j:2 * j + 2]).then_inc(x_in[j], 16)
                for e in range(2):
                    act.wait_ge(o_out[e], 16 * 8 * (layer + 1))
                for k in range(4):
                    act.dma_start(raw[:, k], dO[k]).then_inc(o_in[k], 16)
                for k in range(8):
                    act.wait_ge(o_in[k % 4], 16 * (2 * layer + k // 4 + 1))
                    nc.scalar.activation(H[:, k, 0], raw[:, k % 4], ACT.Copy).then_inc(o_hi, 1)
                    if 1 <= k <= 4:
                        act.wait_ge(o_lo, 8 * layer + k)
                        act.dma_start(raw[:, k - 1], dO[k + 3]).then_inc(o_in[k - 1], 16)

            def ffn(layer):
                u0, d0 = 2 * FT * layer, 88 * layer

                def tap(s, gv, tile, ut, low_need=None):
                    act.wait_ge(up_ps, ut + 1)
                    if low_need is not None:
                        act.wait_ge(hid_lo, low_need)
                    dst = (cG if gv == 0 else cV)[:, s]
                    par = conv_s[:, layer, :, :]
                    nc.scalar.activation(dst, pair(2 * gv), ACT.Identity, scale=par[:, tile, 2:3].rearrange("p a b -> p (a b)"),
                                         bias=par[:, tile, 3:4].rearrange("p a b -> p (a b)")).then_inc(cv0, 1)

                def silu(s, ut):
                    act.wait_ge(cv2, ut + 1)
                    nc.scalar.activation(cG[:, s], cG[:, s], ACT.Silu).then_inc(silu_done, 1)

                def high(s, jt, dn_need):
                    act.wait_ge(prod, jt + 1)
                    if dn_need is not None:
                        act.wait_ge(dn_ps, dn_need)
                    nc.scalar.activation(hid[:, s, 0], cV[:, s], ACT.Copy).then_inc(hid_hi, 1)

                def load_ada(chunk):
                    w_, n0 = chunk
                    act.dma_start(ada_raw_f[:], w_.rearrange("(k p) n -> p k n", p=P)[:, :, n0:n0 + 1024] if isinstance(n0, int)
                                  else w_.rearrange("(k p) n -> p k n", p=P)[:, :, bass.ds(n0, 1024)]).then_inc(ada_in, 16)

                def body(it, dn_need, ada):
                    for s in range(2):
                        ut = it * 4 + (u0 + 2 * s)
                        j = it * 2 + s
                        tap(s, 0, bass.ds(j, 1), ut)
                        silu(s, ut)
                        tap(s, 1, bass.ds(j + FT, 1), ut + 1,
                            None if dn_need is None else it * 2 + (FT * layer + s - 1))
                        high(s, it * 2 + (FT * layer + s), dn_need)
                        if s == 0 and ada is not None:
                            act.wait_ge(ada_step, ada[1])
                            load_ada(ada[0])

                if layer == 0:
                    act.wait_ge(h_lo, 16)
                    load_ada((kv_ada_w, 0))
                body(0, None, None)
                if layer == 0:
                    body(1, 8, ((kv_ada_w, 1024), 104))
                    with act.Fori(2, 8) as it:
                        body(it, it * 8, ((ada_w[1], it * 1024 - 2048), it * 8 + 96))
                    with act.Fori(8, 11) as it:
                        body(it, it * 8, None)
                else:
                    with act.Fori(1, 11) as it:
                        body(it, it * 8 + d0, None)

            out_proj(0, x_t)
            for k in range(8):
                squares(1)(k)
            root(1)
            modulate(1)
            ffn(0)
            for k in range(8):
                squares(2)(k)
            act.dma_start(dX.rearrange("k p s -> p k s"), X[:]).then_inc(x_out, 16)
            root(2)
            modulate(2)
            for n in range(4):
                act.wait_ge(kb_ps, n + 1)
                for e in range(2):
                    rows = bank(n)[64 * e:64 * e + 64]
                    gk = 2 * (n // 2) + e
                    cols = slice(PAD + n % 2 * HALF, PAD + n % 2 * HALF + HALF)
                    nc.scalar.activation(KSB[64:128, gk, cols], rows, ACT.Copy)
                    last = nc.scalar.activation(KSB[0:64, gk, cols], rows, ACT.Copy)
                last.then_inc(kb_hi, 1)
            for tt in range(8):
                act.wait_ge(kb_ps, 4 + tt + 1)
                nc.scalar.activation(VB[:, tt, :, 0, :], bank(4 + tt % 4, 0, 256).rearrange("p (h d) -> p h d", h=4),
                                     ACT.Copy).then_inc(kb_hi, 1)
            modulate(3)
            act.wait_ge(x_out, 16)
            act.wait_ge(h_lo, 32)
            act.wait_ge(kb_lo, 12)
            act.dma_start(VBs[64:128].bitcast(F32), VB[0:64].bitcast(F32)).then_inc(vs_in, 16)
            act.dma_start(VBs[0:64, 1:8].bitcast(F32), VB[64:128, 0:7].bitcast(F32)).then_inc(vs_in, 16)
            act.dma_start(bias_s[:], alibi).then_inc(vs_in, 16)

            def q_high(hp, hh):
                act.wait_ge(qB_ps, 2 * hp + hh + 1)
                for e in range(2):
                    rows = bank(6 + hh)[64 * e:64 * e + 64].rearrange("p (n q) -> p n q", q=CH)
                    last = nc.scalar.activation(QB[0:64, hp % 2, 8 * hh:8 * hh + 8, e, :], rows, ACT.Copy,
                                                scale=QSCALE)
                last.then_inc(qB_hi, 1)

            q_high(0, 0)
            q_high(0, 1)
            for u in range(34):
                if u < 32:
                    hp = u // 4
                    act.wait_ge(mB, u + 1)
                    for j in range(4):
                        nc.scalar.activation(PB[:, u % 2, j, :], PB[:, u % 2, j, :], ACT.Exp,
                                             bias=nmB[:, u % 2, j:j + 1], accum_out=dnB[:, u % 2, j:j + 1])
                    nc.scalar.activation(esB[:, u % 2], nmB[:, u % 2], ACT.Exp,
                                         bias=sink_s[:, hp:hp + 1]).then_inc(expB, 1)
                if u < 28 and u % 2:
                    q_high(u // 4 + 1, u % 4 // 2)
                if u >= 2:
                    v = u - 2
                    act.wait_ge(pvB_ps, v + 1)
                    for e in range(2):
                        if 2 * v + e >= 2:
                            act.wait_ge(o_addB, 2 * v + e - 1)
                        src = bank(4 + v % 2)[64 - 64 * e:128 - 64 * e].rearrange("p (n e q) -> p n e q", e=2, q=CH)
                        nc.scalar.activation(O_tmpB[64 * e:64 * e + 64], src[:, :, e, :], ACT.Copy).then_inc(o_tmpB, 1)
                    if v % 4 == 3:
                        hp = v // 4
                        act.wait_ge(o_addB, 2 * v + 2)
                        for e in range(2):
                            act.dma_start(dO[hp, 64 * e:64 * e + 64, :], O_stB[64 * e:64 * e + 64]).then_inc(o_out[e], 16)
                if 1 <= u <= 32:
                    act.wait_ge(tB_ps, u)
                    if u >= 2:
                        act.wait_ge(pvB_ps, u - 1)
                    nc.scalar.activation(PTB[:, 0], bank(2 + (u - 1) % 2), ACT.Copy).then_inc(ptB_hi, 1)

            out_proj(1, dX)
            for k in range(8):
                squares(3)(k)
            root(3)
            modulate(4)
            ffn(1)
            for k in range(8):
                squares(4)(k)
            root(4)
            for k in range(8):
                act.wait_ge(t_done, 40 + k + 1)
                if k >= 2:
                    act.wait_ge(y_out[k % 2], 16 * (k // 2))
                nc.scalar.activation(hf[:, k % 2], tn[:, k % 2], ACT.Copy,
                                     scale=gain[:, G_FIN + k:G_FIN + k + 1]).then_inc(y_done, 1)
                act.wait_ge(y_done, k + 1)
                act.dma_start(out_t[k], hf[:, k % 2]).then_inc(y_out[k % 2], 16)
            for e in range(2):
                act.wait_ge(y_out[e], 64)

        @block.vector
        def _(dve):
            V_ = nc.vector

            def add_squares(n):
                def one(k):
                    dve.wait_ge(sq_done, 8 * n + k + 1)
                    if k == 0:
                        V_.tensor_copy(ss[:], sq[:, 0]).then_inc(ss_done, 1)
                    else:
                        dve.wait_ge(ss_done, 8 * n + k)
                        V_.tensor_tensor(ss[:], ss[:], sq[:, k % 2], ALU.add).then_inc(ss_done, 1)
                return one

            def inverse_root(n):
                dve.wait_ge(rt_done, n + 1)
                V_.reciprocal(rstd[:], rt[:]).then_inc(rs_done, 1)
                dve.wait_ge(rs_done, n + 1)

            def coefficients(hn):
                gc, sc, _ = MODS[hn]
                V_.scalar_tensor_tensor(coef[:, 8 * hn:8 * hn + 8], mods[:, sc:sc + 8], 1.0, gain[:, gc:gc + 8],
                                        ALU.add, ALU.mult)

            def scaled(hn, k, free):
                if k >= 2:
                    dve.wait_ge(free, (8 * hn if hn < 5 else 0) + k - 1)
                V_.tensor_tensor(tn[:, k % 2], X[:, k], rstd[:], ALU.mult).then_inc(t_done, 1)

            def low(hn, k):
                dve.wait_ge(h_hi, 8 * hn + k + 1)
                V_.tensor_tensor(H[:, k, 1], hf[:, k % 2], H[:, k, 0].bitcast(F32), ALU.subtract).then_inc(h_lo, 1)

            def modulate(hn):
                for k in range(KT + 1):
                    if k < KT:
                        scaled(hn, k, h_hi)
                    if k:
                        low(hn, k - 1)

            def ada_steps(acc, raw, first, n0=0, ks=range(KT)):
                for k in ks:
                    if k == 0:
                        V_.tensor_scalar(acc, raw(k), c_act[:, 0:1], None, ALU.mult).then_inc(ada_step, 1)
                    else:
                        dve.wait_ge(ada_step, first + k)
                        V_.scalar_tensor_tensor(acc, raw(k), c_act[:, k:k + 1], acc, ALU.mult,
                                                ALU.add).then_inc(ada_step, 1)

            V_.memset(eps_s[:], EPS)
            V_.memset(one_s[:], 1.0)
            V_.memset(ones[:], 1.0 / D).then_inc(set_done, 1)
            dve.wait_ge(cact_done, 1)
            for j in range(4):
                dve.wait_ge(ada0_in[j], 16)
                ada_steps(ada_acc0[:, j], lambda k: ada_raw0[:, j, k, :], 8 * j)
                dve.wait_ge(ada_ps, j + 1)
                V_.tensor_tensor(mods[:, 4 * j:4 * j + 4], bank(PV_BANK, 0, 4), modb[:, 4 * j:4 * j + 4],
                                 ALU.add).then_inc(ada_ev, 1)
                add_squares(0)(2 * j)
                add_squares(0)(2 * j + 1)
            dve.wait_ge(ada_ev, 4)
            coefficients(0)
            inverse_root(0)
            modulate(0)
            dve.wait_ge(const_r, 1)
            V_.tensor_tensor(wf[:, 1], wf_raw[:], wf[:, 0].bitcast(F32), ALU.subtract).then_inc(z_v, 1)
            dve.wait_ge(z_ps, 1)
            V_.tensor_tensor(zb[:], bank(2, 0, 128).rearrange("p (t h) -> p t h", h=16),
                             bf_s[:, None, :].to_broadcast([P, 8, 16]), ALU.add).then_inc(z_v, 1)
            dve.wait_ge(z_v, 2)
            V_.scalar_tensor_tensor(za[:], zb[:], -1.0, zb[:], ALU.mult, ALU.max).then_inc(z_v, 1)
            dve.wait_ge(z_v, 3)
            V_.tensor_scalar(zb[:], zb[:], 0.0, None, ALU.min).then_inc(z_v, 1)
            dve.wait_ge(z_v, 4)
            dve.wait_ge(z_a, 2)
            V_.tensor_tensor(lf[:], zb[:], zl[:], ALU.subtract).then_inc(z_v, 1)
            dve.wait_ge(f_ps, 1)
            V_.tensor_scalar(nF16[:], BK[0][0:16, 0:2, :].rearrange("p a b -> p (a b)"), -1.0, None,
                             ALU.mult).then_inc(z_v, 1)
            dve.wait_ge(f_out, 16)
            for b in range(2):
                V_.memset(KL[b][64:128].bitcast(F32), 0.0)

            with dve.Fori(0, NG) as g:
                def qk_low(n):
                    pp, is_k, hh = n // 4, n // 2 % 2, n % 2
                    dve.wait_ge(qk_hi, g * 8 + (n + 1))
                    src = bank(n if n < 4 else PJ_BANK)
                    cols = slice(hh * HALF, hh * HALF + HALF)
                    for e in range(2):
                        rows = src[64 * e:64 * e + 64]
                        if is_k:
                            last = V_.tensor_tensor(KL[pp][0:64, e, cols], rows, KS[pp][0:64, e, cols].bitcast(F32),
                                                    ALU.subtract)
                        else:
                            last = V_.scalar_tensor_tensor(QS[pp][64:128, e, cols], rows, QSCALE,
                                                           QS[pp][0:64, e, cols].bitcast(F32), ALU.mult, ALU.subtract)
                    last.then_inc(qk_lo, 1)

                def v_low(tt):
                    dve.wait_ge(v_hi, g * 8 + (tt + 1))
                    V_.tensor_tensor(V[:, tt, :, 1, :], bank(tt % 4, 0, 256).rearrange("p (h d) -> p h d", h=4),
                                     V[:, tt, :, 0, :].bitcast(F32), ALU.subtract).then_inc(v_lo, 1)

                def ada_piece(j):
                    dve.wait_ge(ada_in, g * 32 + 16 * (j + 1))
                    ada_steps(ada_acc_a[:, j], lambda k: ada_raw_a[:, k, :], g * 16 + (32 + 8 * j))

                qk_low(0)
                ada_piece(0)
                for n in range(1, 4):
                    qk_low(n)
                for tt in range(8):
                    v_low(tt)
                    if tt == 4:
                        ada_piece(1)
                dve.wait_ge(ada_ps, g * 2 + 6)
                for j in range(2):
                    V_.tensor_tensor(mods[:, bass.ds(g * 8 + (16 + 4 * j), 4)], bank(PV_BANK, 4 * j, 4 * j + 4),
                                     modb[:, bass.ds(g * 8 + (16 + 4 * j), 4)], ALU.add).then_inc(ada_ev, 1)

                for t in range(34):
                    if 1 <= t <= 32:
                        tau = t - 1
                        n = (tau % 8 + 1) * P
                        dve.wait_ge(exp_done, g * 32 + t)
                        V_.reciprocal(rden[:, tau % 2:tau % 2 + 1], den[:, tau % 2:tau % 2 + 1]).then_inc(rd_done, 1)
                        dve.wait_ge(rd_done, g * 32 + t)
                        V_.tensor_scalar(Pm[:, tau % 2, 0:n], Pm[:, tau % 2, 0:n], rden[:, tau % 2:tau % 2 + 1], None,
                                         ALU.mult).then_inc(p_norm, 1)
                    if t < 32:
                        hl = t // 8
                        n = (t % 8 + 1) * P
                        dve.wait_ge(s_ps, g * 32 + (t + 1))
                        if t >= 2:
                            dve.wait_ge(t_ps, g * 48 + tasks_to(t - 1))
                        if t % 8 == 0:
                            dve.wait_ge(nf_in[hl % 2], g * 32 + 16 * (hl // 2 + 1))
                        V_.tensor_copy(pace[:, 1:2], one_s[:])
                        V_.tensor_tensor_reduce(Pm[:, t % 2, 0:n], pair(2 * (t % 2))[:, 0:n], negF[:, hl % 2, 0:n], 1.0,
                                                NEG, ALU.add, ALU.max, mx[:, t % 2:t % 2 + 1]).then_inc(s_read, 1)
                        dve.wait_ge(s_read, g * 32 + (t + 1))
                        V_.tensor_scalar(nmx[:, t % 2:t % 2 + 1], mx[:, t % 2:t % 2 + 1], -1.0, None,
                                         ALU.mult).then_inc(s_max, 1)
                    if t % 2 and t >= 3:
                        q = (t - 3) // 2
                        e, c = q // 4 % 2, q % 4
                        dve.wait_ge(o_tmp, g * 16 + (q + 1))
                        if q == 8 or q == 12:
                            dve.wait_ge(o_out[e], g * 32 + 16)
                        V_.tensor_tensor(O_st[64 * e:64 * e + 64, c * 256:c * 256 + 256],
                                         bank(PV_BANK, 0, 256)[64 * e:64 * e + 64], O_tmp[64 * e:64 * e + 64],
                                         ALU.add).then_inc(o_add, 1)
                    if t < 16 and t % 4 == 3:
                        qk_low(4 + t // 4)
                    if 1 <= t <= 32:
                        i = tau % 8
                        for j in range(1 if i < 4 else 2):
                            dve.wait_ge(pt_hi, g * 48 + (tasks_to(tau) + j + 1))
                            k0, k1 = 4 * j, min(4 * j + 4, i + 1)
                            cols = slice((tau % 2) * P, (tau % 2) * P + P)
                            V_.tensor_tensor(PT[:, 1, k0:k1, cols],
                                             bank(T_BANK + j, 0, (k1 - k0) * P).rearrange("p (k q) -> p k q", q=P),
                                             PT[:, 0, k0:k1, cols].bitcast(F32), ALU.subtract).then_inc(pt_lo, 1)
                for e in range(2):
                    dve.wait_ge(o_out[e], g * 32 + 32)

            def out_proj(layer):
                n = 1 + 2 * layer
                gc = M_G1 + M_L1 * layer
                for k in range(8):
                    dve.wait_ge(o_hi, 8 * layer + k + 1)
                    V_.tensor_tensor(H[:, k, 1], O_raw[:, k % 4], H[:, k, 0].bitcast(F32),
                                     ALU.subtract).then_inc(o_lo, 1)
                for m in range(8):
                    dve.wait_ge(wo_ps, 8 * layer + m + 1)
                    dve.wait_ge(x_in[m // 2], 32 + 16 * layer)
                    V_.scalar_tensor_tensor(X[:, m], pair(4 + 2 * (m % 2)), mods[:, gc + m:gc + m + 1], X[:, m],
                                            ALU.mult, ALU.add).then_inc(wo_ev, 1)
                    if m:
                        add_squares(n)(m - 1)
                add_squares(n)(7)

            def ffn(layer):
                u0, d0, gc = 2 * FT * layer, 88 * layer, M_G2 + M_L1 * layer

                def taps(s, gv, tile, ut):
                    dst = (cG if gv == 0 else cV)[:, s]
                    src = pair(2 * gv)
                    par = conv_s[:, layer, :, :]
                    dve.wait_ge(cv0, ut + 1)
                    V_.scalar_tensor_tensor(dst[:, 1:S], src[:, 0:S - 1], par[:, tile, 1:2].rearrange("p a b -> p (a b)"),
                                            dst[:, 1:S], ALU.mult, ALU.add).then_inc(cv1, 1)
                    dve.wait_ge(cv1, ut + 1)
                    V_.scalar_tensor_tensor(dst[:, 2:S], src[:, 0:S - 2], par[:, tile, 0:1].rearrange("p a b -> p (a b)"),
                                            dst[:, 2:S], ALU.mult, ALU.add).then_inc(cv2, 1)

                def gated(s, ut, jt):
                    dve.wait_ge(silu_done, jt + 1)
                    dve.wait_ge(cv2, ut + 2)
                    V_.tensor_tensor(cV[:, s], cV[:, s], cG[:, s], ALU.mult).then_inc(prod, 1)

                def low_part(s, jt):
                    dve.wait_ge(hid_hi, jt + 1)
                    V_.tensor_tensor(hid[:, s, 1], cV[:, s], hid[:, s, 0].bitcast(F32), ALU.subtract).then_inc(hid_lo, 1)

                def residual(m, ps_need, self_need):
                    dve.wait_ge(dn_ps, ps_need)
                    if self_need is not None:
                        dve.wait_ge(dn_ev, self_need)
                    V_.scalar_tensor_tensor(X[:, m], pair(4 + 2 * (m % 2)), mods[:, gc + m:gc + m + 1], X[:, m],
                                            ALU.mult, ALU.add).then_inc(dn_ev, 1)

                def body(it, with_down, first_down, ada):
                    for s in range(2):
                        ut = it * 4 + (u0 + 2 * s)
                        j = it * 2 + s
                        jt = it * 2 + (FT * layer + s)
                        taps(s, 0, bass.ds(j, 1), ut)
                        taps(s, 1, bass.ds(j + FT, 1), ut + 1)
                        gated(s, ut, jt)
                        if s == 0 and with_down:
                            if ada is not None:
                                dve.wait_ge(ada_in, ada[0])
                            for m in range(8):
                                need = it * 8 + (d0 - 8 + m + 1)
                                residual(m, need, None if first_down else need - 8)
                                if ada is not None:
                                    ada_steps(ada_acc_f[:], lambda k: ada_raw_f[:, k, :], ada[1], ks=[m])
                        if s == 1 and ada is not None:
                            dve.wait_ge(ada_ps, ada[2])
                            V_.tensor_tensor(mods[:, ada[3]], bank(4, 0, 8), modb[:, ada[3]], ALU.add).then_inc(ada_ev, 1)
                        low_part(s, jt)

                def ada_of(it, cols):
                    return (it * 16 + 128, it * 8 + 88, it + N_ADA_A, cols)

                body(0, False, False, None)
                if layer == 0:
                    body(1, True, True, ada_of(1, slice(M_KV, M_KV + 8)))
                    body(2, True, False, ada_of(2, slice(M_KV + 8, M_KV + 16)))
                    with dve.Fori(3, 9) as it:
                        body(it, True, False, ada_of(it, bass.ds(it * 8 + (M_L1 - 24), 8)))
                    with dve.Fori(9, 11) as it:
                        body(it, True, False, None)
                else:
                    body(1, True, True, None)
                    with dve.Fori(2, 11) as it:
                        body(it, True, False, None)
                for m in range(8):
                    residual(m, d0 + 80 + m + 1, d0 + 72 + m + 1)
                    if m:
                        add_squares(2 + 2 * layer)(m - 1)
                add_squares(2 + 2 * layer)(7)

            out_proj(0)
            dve.wait_ge(ada_ev, N_ADA_A)
            coefficients(1)
            inverse_root(1)
            modulate(1)
            ffn(0)
            dve.wait_ge(ada_ev, N_ADA_A + 8)
            coefficients(2)
            coefficients(3)
            inverse_root(2)
            V_.memset(KSB[:, :, 0:PAD].bitcast(F32), 0.0)
            V_.memset(KLB[0:64, :, 0:PAD].bitcast(F32), 0.0)
            V_.memset(KLB[64:128].bitcast(F32), 0.0)
            modulate(2)
            for n in range(4):
                dve.wait_ge(kb_hi, n + 1)
                for e in range(2):
                    gk = 2 * (n // 2) + e
                    cols = slice(PAD + n % 2 * HALF, PAD + n % 2 * HALF + HALF)
                    last = V_.tensor_tensor(KLB[0:64, gk, cols], bank(n)[64 * e:64 * e + 64],
                                            KSB[0:64, gk, cols].bitcast(F32), ALU.subtract)
                last.then_inc(kb_lo, 1)
            for tt in range(8):
                dve.wait_ge(kb_hi, 4 + tt + 1)
                V_.tensor_tensor(VB[:, tt, :, 1, :], bank(4 + tt % 4, 0, 256).rearrange("p (h d) -> p h d", h=4),
                                 VB[:, tt, :, 0, :].bitcast(F32), ALU.subtract).then_inc(kb_lo, 1)
            modulate(3)
            dve.wait_ge(x_out, 16)
            V_.memset(VBs[0:64, 0].bitcast(F32), 0.0)

            def q_low(hp, hh):
                dve.wait_ge(qB_hi, 2 * hp + hh + 1)
                ch = slice(8 * hh, 8 * hh + 8)
                for e in range(2):
                    rows = bank(6 + hh)[64 * e:64 * e + 64].rearrange("p (n q) -> p n q", q=CH)
                    last = V_.scalar_tensor_tensor(QB[64:128, hp % 2, ch, e, :], rows, QSCALE,
                                                   QB[0:64, hp % 2, ch, e, :].bitcast(F32), ALU.mult, ALU.subtract)
                last.then_inc(qB_lo, 1)

            q_low(0, 0)
            q_low(0, 1)
            dve.wait_ge(vs_in, 48)
            for u in range(34):
                if 1 <= u <= 32:
                    v = u - 1
                    b = v % 2
                    dve.wait_ge(expB, v + 1)
                    V_.tensor_tensor(dnB[:, b], dnB[:, b], esB[:, b], ALU.add).then_inc(dB, 1)
                    dve.wait_ge(dB, 2 * v + 1)
                    V_.reciprocal(rdB[:, b], dnB[:, b]).then_inc(dB, 1)
                    dve.wait_ge(dB, 2 * v + 2)
                    V_.tensor_tensor(PB[:, b], PB[:, b], rdB[:, b, :, None].to_broadcast([P, 4, P]),
                                     ALU.mult).then_inc(pB, 1)
                if u < 32:
                    b, hp = u % 2, u // 4
                    dve.wait_ge(sB_ps, u + 1)
                    if u >= 2:
                        dve.wait_ge(tB_ps, u - 1)
                    for j in range(4):
                        if u % 4 == 0 and j == 0:
                            V_.memset(PB[:, b, 0, 0:CH], NEG)
                            last = V_.tensor_tensor_reduce(PB[:, b, j, CH:P], bank(b, CH, P), bias_s[:, hp, CH:P],
                                                           1.0, NEG, ALU.add, ALU.max, mxB[:, b, j:j + 1])
                        else:
                            last = V_.tensor_tensor_reduce(PB[:, b, j, :], bank(b, j * P, j * P + P), bias_s[:, hp, :],
                                                           1.0, NEG, ALU.add, ALU.max, mxB[:, b, j:j + 1])
                    last.then_inc(sB_read, 1)
                    dve.wait_ge(sB_read, u + 1)
                    V_.tensor_scalar(nmB[:, b], mxB[:, b], sink_s[:, hp:hp + 1], -1.0, ALU.max, ALU.mult).then_inc(mB, 1)
                if u < 28 and u % 2:
                    q_low(u // 4 + 1, u % 4 // 2)
                if u >= 2:
                    v = u - 2
                    if v % 4 == 0 and v:
                        for e in range(2):
                            dve.wait_ge(o_out[e], 128 + 16 * (v // 4))
                    dve.wait_ge(o_tmpB, 2 * v + 2)
                    for e in range(2):
                        src = bank(4 + v % 2)[64 * e:64 * e + 64].rearrange("p (n e q) -> p n e q", e=2, q=CH)
                        dst = O_stB[64 * e:64 * e + 64, v % 4 * 256:v % 4 * 256 + 256].rearrange("p (n q) -> p n q", q=CH)
                        V_.tensor_tensor(dst, src[:, :, e, :], O_tmpB[64 * e:64 * e + 64], ALU.add).then_inc(o_addB, 1)
                if 1 <= u <= 32:
                    dve.wait_ge(ptB_hi, u)
                    V_.tensor_tensor(PTB[:, 1], bank(2 + (u - 1) % 2), PTB[:, 0].bitcast(F32),
                                     ALU.subtract).then_inc(ptB_lo, 1)

            out_proj(1)
            coefficients(4)
            inverse_root(3)
            modulate(4)
            ffn(1)
            inverse_root(4)
            for k in range(8):
                scaled(5, k, y_done)


INPUTS = ["x_t", "c_t", "ada_w", "kv_ada_w", "mod_b", "gains", "w_stream", "w_f", "b_f", "sinks", "conv",
          "ident", "mask", "stair", "alibi"]


def layout(i):
    f = np.float32
    a = {k: np.asarray(v) for k, v in i.items()}

    def stationary(w, m):
        return w[:, m * P:m * P + P].reshape(KT, P, P).transpose(1, 0, 2).reshape(P, 1024)

    def moving(w, n0):
        t = w[:, n0:n0 + 256].reshape(2, 4, P, 256).transpose(0, 2, 1, 3).reshape(2, P, 1024)
        return [t[0], t[1]]

    w_in = a["a_w_in"][0]
    wq, wk, wv = w_in[:, 0:D], w_in[:, D:2 * D], w_in[:, 2 * D:3 * D]
    tiles = []
    for g in range(NG):
        tiles += [stationary(wq, 2 * g), stationary(wk, 2 * g)]
        tiles += moving(wv, 256 * g)
        tiles += [stationary(wq, 2 * g + 1), stationary(wk, 2 * g + 1)]
    tiles += [stationary(a["a_w_o"][0], m) for m in range(8)]

    def ffn(l):
        up, dn = a["ffn_w_up"][l], a["ffn_w_down"][l]
        ups = lambda j: [stationary(up, j), stationary(up, FT + j)]
        out = ups(0) + ups(1)
        for it in range(1, FT // 2):
            out += ups(2 * it) + [dn[(2 * it - 2) * P:(2 * it - 1) * P], dn[(2 * it - 1) * P:2 * it * P]] + ups(2 * it + 1)
        return out + [dn[(FT - 2) * P:(FT - 1) * P], dn[(FT - 1) * P:]]

    tiles += ffn(0)
    tiles += [stationary(a["kv_w"], m) for m in range(2)] + moving(a["kv_w"], KV * HD)
    tiles += [stationary(a["b_w_q"][0], m) for m in range(8)]
    tiles += [stationary(a["b_w_o"][0], m) for m in range(8)]
    tiles += ffn(1)
    cols = lambda v: np.asarray(v).reshape(-1, P).T
    conv = np.stack([np.stack([cols(a["ffn_conv_w"][l][j]) for j in range(3)] + [cols(a["ffn_conv_b"][l])], axis=-1)
                     for l in range(2)], axis=1)
    r = np.arange(P)
    mask = np.where(r[None, :] <= r[:, None], 0.0, NEG).astype(f)
    stair = (np.arange(S)[None, :] >= r[:, None]).astype(f)
    slopes = np.exp2(-8.0 * (np.arange(NH, dtype=f) + 1.0) / NH).astype(f)
    dist = np.abs(np.arange(CH)[:, None] + CH - np.arange(2 * CH)[None, :]).astype(f)
    alibi = -(slopes.reshape(8, 2)[:, :, None, None] * dist[None, None]).reshape(8, P, P).transpose(1, 0, 2)
    return {
        "x_t": a["x"][0].T.reshape(KT, P, S), "c_t": cols(a["c"][0]), "ada_w": a["ada_w"],
        "kv_ada_w": a["kv_ada_w"],
        "mod_b": np.concatenate([cols(a["ada_b"][0]), cols(a["ada_b"][1]), cols(a["kv_ada_b"])], axis=1),
        "gains": np.concatenate([cols(v) for v in (a["norm1_g"][0], a["norm1_g"][1], a["norm2_g"][0],
                                                   a["norm2_g"][1], a["kv_norm_g"], a["final_g"])], axis=1),
        "w_stream": np.stack(tiles), "w_f": w_in[:, 3 * D:].reshape(KT, P, NH).transpose(1, 0, 2),
        "b_f": np.broadcast_to(a["a_b_f"][0], (P, NH)),
        "sinks": np.repeat(a["b_sinks"][0].reshape(8, 2).T, CH, axis=0),
        "conv": conv, "ident": np.eye(P, dtype=f), "mask": mask, "stair": stair, "alibi": alibi,
    }


def kernel(**inputs):
    import concourse.bacc as bacc
    from concourse.bass_utils import run_bass_kernel_spmd as run

    nc = bacc.Bacc("TRN2", target_bir_lowering=False, num_devices=1)
    arrays, args = {}, []
    laid = layout(inputs)
    for name in INPUTS:
        v = np.ascontiguousarray(laid[name])
        arrays[f"in_{name}"] = v
        args.append(nc.dram_tensor(f"in_{name}", v.shape, mybir.dt.from_np(v.dtype), kind="ExternalInput").ap())
    args.append(nc.dram_tensor("out_0", (KT, P, S), F32, kind="ExternalOutput").ap())
    program(nc, *args)
    r = run(nc, [arrays], core_ids=[0])
    return r.results[0]["out_0"].reshape(D, S).T.reshape(1, S, D)
```

```python
from contextlib import ExitStack

import numpy as np

import concourse.bass as bass
from concourse import mybir

F32 = mybir.dt.float32
F32R = mybir.dt.float32r
ALU = mybir.AluOpType
ACT = mybir.ActivationFunctionType

P = 128
D = 1024
S = 1024
HALF = 512
KT = D // P
HD = 64
NH = D // HD
KV = 4
CH = 64
FF = 2816
FT = FF // P
NG = 4
EPS = 1e-6
NEG = -1e30
QSCALE = 1.0 / 8.0

W_ATT_A = 0
W_OUT_A = W_ATT_A + 6 * NG
W_FFN = [W_OUT_A + 8, 0]
W_KV = W_FFN[0] + 3 * FT
W_Q_B = W_KV + 4
W_OUT_B = W_Q_B + 8
W_FFN[1] = W_OUT_B + 8
W_TILES = W_FFN[1] + 3 * FT
RAW = 2
SPL = 3

M_SH1, M_SC1, M_G1, M_SH2, M_SC2, M_G2 = (8 * i for i in range(6))
M_L1 = 48
M_KV = 96
G_N1, G_N2, G_KV, G_FIN = 0, 16, 32, 40


def tasks_before(i):
    return i if i <= 4 else 2 * i - 4


def tasks_to(t):
    return 12 * (t // 8) + tasks_before(t % 8)


def task_bank(task):
    first = tasks_to(14)
    return (4, 5)[task % 2] if task < first else (4, 5, 7)[(task - first) % 3]


def last_in_bank(task):
    return next((n for n in range(task - 1, -1, -1) if task_bank(n) == task_bank(task)), None)


def program(nc, x_t, c_t, ada_w, kv_ada_w, mod_b, gains, w_stream, w_f, b_f, sinks, conv, ident, mask,
            stair, alibi, out_t):
    ctx = ExitStack()
    with ctx:
        base = (nc.sbuf_base + 63) // 64 * 64
        K_ = 1024

        def at(name, shape, dt, kb):
            return nc.alloc_sbuf_tensor_at(name, shape, dt, offset=base + int(kb * K_))

        def sem(name):
            return ctx.enter_context(nc.semaphore(name))

        H = at("H", [P, KT, 2, S], F32R, 0)
        ada_raw0 = at("ada_raw0", [P, 4, KT, 512], F32, 0)
        X = at("X", [P, KT, S], F32, 64)
        w_raw = at("w_raw", [P, RAW, 1024], F32, 96)
        w_spl = at("w_spl", [P, SPL, 2, 1024], F32R, 104)
        QS = [at("QS0", [P, 2, S], F32R, 64), at("QS1", [P, 2, S], F32R, 128)]
        KS = [at("KS0", [P, 2, S], F32R, 72), at("KS1", [P, 2, S], F32R, 136)]
        KL = [at("KL0", [P, 2, S], F32R, 80), at("KL1", [P, 2, S], F32R, 144)]
        negF = at("negF", [P, 2, S], F32, 88)
        V = at("V", [P, 8, 4, 2, HD], F32R, 152)
        Pm = [at(f"Pm{i}", [P, S], F32, kb) for i, kb in enumerate((168, 172, 196))]
        ada_acc_a = at("ada_acc_a", [P, 2, 512], F32, 168)
        O_raw = at("O_raw", [P, 4, S], F32, 168)
        PT = at("PT", [P, 2, 8, 256], F32R, 176)
        ada_raw_a = at("ada_raw_a", [P, KT, 512], F32, 176)
        O_st = at("O_st", [P, S], F32, 192)
        O_tmp = at("O_tmp", [P, 256], F32, 206.125)
        zb = at("zb", [P, 8, 16], F32, 128)
        za = at("za", [P, 8, 16], F32, 128.5)
        ze = at("ze", [P, 8, 16], F32, 129)
        zl = at("zl", [P, 8, 16], F32, 129.5)
        lf = at("lf", [P, 8, 16], F32, 130)
        wf_raw = at("wf_raw", [P, KT, 16], F32, 130.5)
        wf = at("wf", [P, 2, KT, 16], F32R, 131)
        stair_s = at("stair_s", [P, S], F32, 132)
        zt = at("zt", [16, S], F32, 160)
        ada_acc0 = at("ada_acc0", [P, 4, 512], F32, 164)
        nF16 = at("nF16", [16, S], F32, 136)
        mask_f = at("mask_f", [P, P], F32, 140)
        sq = at("sq", [P, 2, S], F32, 144)
        ss = at("ss", [P, S], F32, 152)
        diag = at("diag", [P, KT, P], F32, 156)
        rstd = at("rstd", [P, S], F32, 180)
        tn = at("tn", [P, 2, S], F32, 184)
        hf = at("hf", [P, 2, S], F32, 192)
        hid = at("hid", [P, 2, 2, S], F32R, 128)
        cG = at("cG", [P, 2, S], F32, 144)
        cV = at("cV", [P, 2, S], F32, 152)
        ada_raw_f = at("ada_raw_f", [P, KT, 1024], F32, 160)
        ada_acc_f = at("ada_acc_f", [P, 1024], F32, 192)
        PAD = CH
        KSB = at("KSB", [P, KV, PAD + S], F32R, 128)
        KLB = at("KLB", [P, KV, PAD + S], F32R, 145)
        VB = at("VB", [P, 8, KV, 2, HD], F32R, 162)
        VBs = at("VBs", [P, 8, KV, 2, HD], F32R, 64)
        QB = at("QB", [P, 2, S // CH, 2, CH], F32R, 80)
        PB = [at(f"PB{i}", [P, 4, P], F32, kb) for i, kb in enumerate((178, 180, 196))]
        PTB = at("PTB", [P, 2, 512], F32R, 182)
        bias_s = at("bias_s", [P, 8, P], F32, 186)
        O_stB = at("O_stB", [P, S], F32, 190)
        O_tmpB = at("O_tmpB", [P, 4, CH], F32, 194)
        id_f = at("id_f", [P, P], F32, 200)
        id_r = at("id_r", [P, P], F32R, 200.5)
        mask_r = at("mask_r", [P, P], F32R, 201)
        ones = at("ones", [P, P], F32, 201.5)
        mods = at("mods", [P, 112], F32, 202)
        modb = at("modb", [P, 112], F32, 202.5)
        gain = at("gain", [P, 48], F32, 203)
        coef = at("coef", [P, 48], F32, 203.25)
        conv_s = at("conv_s", [P, 2, 2 * FT, 4], F32, 203.5)
        bf_s = at("bf_s", [P, 16], F32, 205)
        sink_s = at("sink_s", [P, 8], F32, 205.125)
        c_s = at("c_s", [P, KT], F32, 205.1875)
        c_act = at("c_act", [P, KT], F32, 205.25)
        eps_s = at("eps_s", [P, 1], F32, 205.3125)
        one_s = at("one_s", [P, 1], F32, 205.375)
        pace = at("pace", [P, 2], F32, 206)
        rt = at("rt", [P, KT], F32, 206.03125)
        rs = at("rs", [P, KT], F32, 206.0625)
        mx = at("mx", [P, 2], F32, 205.4375)
        nmx = at("nmx", [P, 2], F32, 205.5)
        den = at("den", [P, 2], F32, 205.5625)
        rden = at("rden", [P, 2], F32, 205.625)
        mxB = at("mxB", [P, 2, 4], F32, 205.6875)
        nmB = at("nmB", [P, 2, 4], F32, 205.75)
        dnB = at("dnB", [P, 2, 4], F32, 205.8125)
        esB = at("esB", [P, 2, 4], F32, 205.875)
        rdB = at("rdB", [P, 2, 4], F32, 205.9375)

        BK = [ctx.enter_context(nc.psum_tensor(f"bank{i}", [P, 4, HALF], F32)) for i in range(2)]

        def bank(i, lo=0, hi=HALF):
            return BK[i // 4][:, i % 4, lo:hi]

        def pair(i):
            return BK[i // 4][:, i % 4:i % 4 + 2, :].rearrange("p a b -> p (a b)")

        PV_BANK, PJ_BANK = 6, 7

        dO = nc.dram_tensor("scratch_o", [8, P, S], F32).ap()
        dX = nc.dram_tensor("scratch_x", [KT, P, S], F32).ap()
        dF = nc.dram_tensor("scratch_f", [16, S], F32).ap()

        raw_in = [sem(f"raw_in{i}") for i in range(RAW)]
        w_hi = sem("w_hi")
        w_ready = sem("w_ready")
        w_used = sem("w_used")
        const_in = sem("const_in")
        gate_in = sem("gate_in")
        cact_done = sem("cact_done")
        set_done = sem("set_done")
        ada0_in = [sem(f"ada0_in{i}") for i in range(4)]
        ada_in = sem("ada_in")
        ada0_step = sem("ada0_step")
        ada_step = sem("ada_step")
        ada_ps = sem("ada_ps")
        ada_ev = sem("ada_ev")
        x_in = [sem(f"x_in{i}") for i in range(4)]
        sq_done = sem("sq_done")
        ss_done = sem("ss_done")
        ms_ps = sem("ms_ps")
        rt_done = sem("rt_done")
        rs_done = sem("rs_done")
        bc_ps = sem("bc_ps")
        t_done = sem("t_done")
        h_hi = sem("h_hi")
        h_lo = sem("h_lo")
        z_ps = sem("z_ps")
        z_v = sem("z_v")
        z_a = sem("z_a")
        f_ps = sem("f_ps")
        f_out = sem("f_out")
        const_r = sem("const_r")
        nf_in = [sem(f"nf_in{i}") for i in range(2)]
        qk_ps = sem("qk_ps")
        qk_hi = sem("qk_hi")
        qk_lo = sem("qk_lo")
        v_ps = sem("v_ps")
        v_hi = sem("v_hi")
        v_lo = sem("v_lo")
        s_ps = sem("s_ps")
        s_read = sem("s_read")
        s_max = sem("s_max")
        exp_done = sem("exp_done")
        rd_done = sem("rd_done")
        p_norm = sem("p_norm")
        t_ps = sem("t_ps")
        pt_hi = sem("pt_hi")
        pt_lo = sem("pt_lo")
        pv_ps = sem("pv_ps")
        o_tmp = sem("o_tmp")
        o_add = sem("o_add")
        o_out = [sem(f"o_out{i}") for i in range(2)]
        o_in = [sem(f"o_in{i}") for i in range(4)]
        o_hi = sem("o_hi")
        o_lo = sem("o_lo")
        wo_ps = sem("wo_ps")
        wo_ev = sem("wo_ev")
        up_ps = sem("up_ps")
        cv0 = sem("cv0")
        cv1 = sem("cv1")
        cv2 = sem("cv2")
        silu_done = sem("silu_done")
        prod = sem("prod")
        hid_hi = sem("hid_hi")
        hid_lo = sem("hid_lo")
        dn_ps = sem("dn_ps")
        dn_ev = sem("dn_ev")
        x_out = sem("x_out")
        kb_ps = sem("kb_ps")
        vk_ps = sem("vk_ps")
        kb_hi = sem("kb_hi")
        kb_lo = sem("kb_lo")
        vs_in = sem("vs_in")
        sB_ps = sem("sB_ps")
        sB_read = sem("sB_read")
        mB = sem("mB")
        expB = sem("expB")
        dB = sem("dB")
        pB = sem("pB")
        tB_ps = sem("tB_ps")
        ptB_hi = sem("ptB_hi")
        ptB_lo = sem("ptB_lo")
        pvB_ps = sem("pvB_ps")
        o_tmpB = sem("o_tmpB_s")
        o_addB = sem("o_addB")
        qB_ps = sem("qB_ps")
        qB_hi = sem("qB_hi")
        qB_lo = sem("qB_lo")
        y_done = sem("y_done")
        y_out = [sem(f"y_out{i}") for i in range(2)]

        N_ADA_A = 4 + 2 * NG
        NORM_IN = [None, (wo_ev, 0), (dn_ev, 80), (wo_ev, 8), (dn_ev, 88 + 80)]
        MODS = [(G_N1, M_SC1, M_SH1), (G_N2, M_SC2, M_SH2), (G_KV, M_KV + 8, M_KV),
                (G_N1 + 8, M_L1 + M_SC1, M_L1 + M_SH1), (G_N2 + 8, M_L1 + M_SC2, M_L1 + M_SH2)]

        def q_bank(hp, hh):
            return 6 + hh if hp else hh

        block = ctx.enter_context(nc.Block())

        @block.sync
        def _(sp):
            for dst, src in ((c_s, c_t), (modb, mod_b), (gain, gains), (bf_s, b_f), (sink_s, sinks),
                             (id_f, ident), (conv_s, conv)):
                sp.dma_start(dst[:], src).then_inc(const_in, 16)
            for j in range(4):
                sp.dma_start(X[:, 2 * j:2 * j + 2], x_t.rearrange("k p s -> p k s")[
                    :, 2 * j:2 * j + 2]).then_inc(x_in[j], 16)
            for dst, src in ((wf_raw, w_f), (stair_s, stair), (mask_f, mask)):
                sp.dma_start(dst[:], src).then_inc(gate_in, 16)
            for j in range(4):
                sp.dma_start(ada_raw0[:, j], ada_w[0].rearrange("(k p) n -> p k n", p=P)[
                    :, :, 512 * j:512 * j + 512]).then_inc(ada0_in[j], 16)

            def load(pos, u, free):
                if free is not None:
                    sp.wait_ge(w_ready, free)
                sp.dma_start(w_raw[:, u % RAW, :], w_stream[pos]).then_inc(raw_in[u % RAW], 16)

            for u in range(6):
                load(u, u, u - 1 if u >= RAW else None)
            with sp.Fori(1, W_TILES // 6) as it:
                for u in range(6):
                    load(it * 6 + u, u, it * 6 + u - 1)
            for pos in range(W_TILES // 6 * 6, W_TILES):
                load(pos, pos, pos - 1)

        @block.gpsimd
        def _(pool):
            def split(pos, u, raw_value, free):
                pool.wait_ge(raw_in[u % RAW], raw_value)
                if free is not None:
                    pool.wait_ge(w_used, free)
                pool.tensor_tensor(pace[:, 0:1], one_s[:], one_s[:], ALU.mult)
                hi, lo = w_spl[:, u % SPL, 0, :], w_spl[:, u % SPL, 1, :]
                pool.tensor_scalar(hi, w_raw[:, u % RAW, :], 1.0, 1.0, ALU.mult, ALU.mult).then_inc(w_hi, 1)
                pool.wait_ge(w_hi, pos + 1)
                pool.tensor_tensor(lo, w_raw[:, u % RAW, :], hi.bitcast(F32), ALU.subtract).then_inc(w_ready, 1)

            pool.wait_ge(set_done, 1)
            for u in range(6):
                split(u, u, 16 * (u // RAW + 1), u - SPL + 1 if u >= SPL else None)
            with pool.Fori(1, W_TILES // 6) as it:
                for u in range(6):
                    split(it * 6 + u, u, it * 48 + 16 * (u // RAW + 1), it * 6 + (u - SPL + 1))
            for pos in range(W_TILES // 6 * 6, W_TILES):
                split(pos, pos, 16 * (pos // RAW + 1), pos - SPL + 1)

        @block.tensor
        def _(pe):
            def product(dst, stat, mov, ks=range(KT), release=0):
                for k in ks:
                    for a, b in ((0, 0), (0, 1), (1, 0)):
                        last = pe.matmul(dst, stat(k, a), mov(k, b), start=(k == 0 and a + b == 0),
                                         stop=(k == KT - 1 and a == 1))
                        if release:
                            last.then_inc(w_used, release)
                            release = 0
                return last

            def h_cols(lo, n):
                return lambda k, part: H[:, k, part, lo:lo + n]

            def w_tile(u):
                return lambda k, part: w_spl[:, u % SPL, part, k * P:k * P + P]

            def ada_cols(acc, cols, need, slot_bank, col0, steps=ada_step):
                pe.wait_ge(steps, need)
                for j in range(cols):
                    last = pe.matmul(bank(slot_bank, col0 + j, col0 + j + 1), acc[:, j * P:j * P + P],
                                     one_s[:], start=True, stop=True)
                last.then_inc(ada_ps, 1)

            def mean_squares(n, release=0):
                pe.wait_ge(ss_done, 8 * n + 8)
                for b in range(8):
                    last = pe.matmul(bank(0, b, b + 1), ss[:, b * P:b * P + P], ones[:, 0:1], start=True, stop=True)
                    if b == 0 and release:
                        last.then_inc(w_used, release)
                last.then_inc(ms_ps, 1)
                pe.wait_ge(rs_done, 3 * n + 2)
                for hh in range(2):
                    last = pe.matmul(bank(hh), ones[:], diag[:, 4 * hh:4 * hh + 4].rearrange("p a b -> p (a b)"),
                                     start=True, stop=True)
                last.then_inc(bc_ps, 1)

            pe.wait_ge(set_done, 1)
            mean_squares(0)
            for j in range(4):
                if j:
                    pe.wait_ge(ada_ev, j)
                ada_cols(ada_acc0[:, j], 4, 8 * (j + 1), PV_BANK, 0, ada0_step)
            pe.wait_ge(z_v, 1)
            for k in range(KT):
                pe.wait_ge(h_lo, k + 1)
                for hh in range(2):
                    for a, b in ((0, 0), (0, 1), (1, 0)):
                        last = pe.matmul(bank(2 + hh)[0:16], wf[:, a, k, :], H[:, k, b, hh * HALF:hh * HALF + HALF],
                                         start=(k == 0 and a + b == 0), stop=(k == KT - 1 and a == 1))
            last.then_inc(z_ps, 1)
            pe.wait_ge(z_v, 2)
            for tt in range(8):
                last = pe.transpose(bank(4, tt * 16, tt * 16 + 16), zt[:, tt * P:tt * P + P], id_f[0:16, 0:16])
            last.then_inc(z_ps, 1)
            pe.wait_ge(z_v, 6)
            for hh in range(2):
                for t in range(4 * hh + 4):
                    lo = max(t * P, hh * HALF)
                    last = pe.matmul(bank(hh, lo - hh * HALF, HALF)[0:16], lf[:, t, :],
                                     stair_s[:, lo - t * P:(hh + 1) * HALF - t * P], start=(t == 0),
                                     stop=(t == 4 * hh + 3))
            last.then_inc(f_ps, 1)
            pe.wait_ge(z_v, 7)

            with pe.Fori(0, NG) as g:
                for n in range(4):
                    u = n // 2
                    if n % 2 == 0:
                        pe.wait_ge(w_ready, g * 6 + (u + 1))
                    last = product(bank(n), w_tile(u), h_cols((n % 2) * HALF, HALF), release=int(n == 2))
                    last.then_inc(qk_ps, 1)
                pe.wait_ge(w_ready, g * 6 + 4)
                for tt in range(8):
                    if tt < 4:
                        pe.wait_ge(qk_lo, g * 8 + (tt + 1))
                    else:
                        pe.wait_ge(v_lo, g * 8 + (tt - 3))
                    last = product(bank(tt % 4, 0, 256), lambda k, a: H[:, k, a, tt * P:tt * P + P],
                                   lambda k, b: w_spl[:, 2 - k // 4 * 2, b, (k % 4) * 256:(k % 4) * 256 + 256],
                                   release=int(tt == 0))
                    last.then_inc(v_ps, 1)
                for j in range(2):
                    ada_cols(ada_acc_a[:, j], 4, g * 16 + 8 * (j + 1), PV_BANK, 4 * j)
                pe.wait_ge(v_lo, g * 8 + 8)
                pe.wait_ge(ada_ev, g * 2 + 6)

                def scores(t):
                    pp, e, i = t // 16, t // 8 % 2, t % 8
                    if t % 16 == 0:
                        pe.wait_ge(qk_lo, g * 8 + (4 + 4 * pp))
                    if t >= 2:
                        pe.wait_ge(s_read, g * 32 + (t - 1))
                    n = (i + 1) * P
                    for c0 in range(0, n, HALF):
                        m = min(HALF, n - c0)
                        dst = bank(2 * (t % 2) + c0 // HALF, 0, m)
                        q = QS[pp][:, e, i * P:i * P + P]
                        first = pe.matmul(dst, q, KS[pp][:, e, c0:c0 + m], start=True, stop=False)
                        if t == 16:
                            first.then_inc(w_used, 1)
                        last = pe.matmul(dst, q, KL[pp][:, e, c0:c0 + m], start=False, stop=True)
                        if c0 + m == n:
                            last = pe.matmul(bank(2 * (t % 2) + c0 // HALF, m - P, m), id_r[:], mask_r[:],
                                             start=False, stop=True, skip_group_check=True)
                    last.then_inc(s_ps, 1)

                def turn(t):
                    pe.wait_ge(p_norm, g * 32 + (t + 1))
                    i = t % 8
                    for j in range(1 if i < 4 else 2):
                        task = tasks_to(t) + j
                        before = last_in_bank(task)
                        if before is not None:
                            pe.wait_ge(pt_lo, g * 48 + (before + 1))
                        kbs = range(4 * j, min(4 * j + 4, i + 1))
                        for kb in kbs:
                            last = pe.transpose(bank(task_bank(task), (kb % 4) * P, (kb % 4) * P + P),
                                                Pm[t % 3][:, kb * P:kb * P + P], id_f[:])
                        last.then_inc(t_ps, 1)

                def values(q):
                    hl, c = q // 4, q % 4
                    pe.wait_ge(pt_lo, g * 48 + tasks_to(2 * q + 2))
                    if q:
                        pe.wait_ge(o_add, g * 16 + q)
                    for kb in range(2 * c + 2):
                        lo = 0 if kb <= 2 * c else P
                        for part in range(2):
                            last = pe.matmul(bank(PV_BANK, lo, 256), V[:, kb, hl, :, :].rearrange("p a b -> p (a b)"),
                                             PT[:, part, kb, lo:256], start=(kb == 0 and part == 0),
                                             stop=(kb == 2 * c + 1 and part == 1), skip_group_check=True)
                    last.then_inc(pv_ps, 1)

                def next_qk(t):
                    n = 4 + t // 4
                    u = 4 + (n - 4) // 2
                    if t % 8 == 0:
                        pe.wait_ge(w_ready, g * 6 + (u + 1))
                    if t % 4 == 0 and n > 4:
                        pe.wait_ge(qk_lo, g * 8 + n)
                    ks = range(2 * (t % 4), 2 * (t % 4) + 2)
                    last = product(bank(PJ_BANK), w_tile(u), h_cols((n % 2) * HALF, HALF), ks,
                                   release={0: 2, 8: 1}.get(t, 0))
                    if t % 4 == 3:
                        last.then_inc(qk_ps, 1)

                for t in range(35):
                    if t < 32:
                        scores(t)
                    if 2 <= t <= 33:
                        turn(t - 2)
                    if t % 2 == 0 and t >= 4:
                        values((t - 4) // 2)
                    if t < 16:
                        next_qk(t)

            def out_proj(layer):
                w0 = [W_OUT_A, W_OUT_B][layer]
                for m in range(8):
                    pe.wait_ge(w_ready, w0 + m + 1)
                    if m >= 2:
                        pe.wait_ge(wo_ev, 8 * layer + m - 1)
                    for k in range(KT):
                        if m == 0:
                            pe.wait_ge(o_lo, 8 * layer + k + 1)
                        for hh in range(2):
                            last = product(bank(4 + 2 * (m % 2) + hh), w_tile(w0 + m), h_cols(hh * HALF, HALF), [k],
                                           release=int(k == 0 and hh == 0 and (m > 0 or layer == 1)))
                    last.then_inc(wo_ps, 1)

            def ffn(layer):
                w0 = W_FFN[layer]
                u0 = 2 * FT * layer

                def first_pair():
                    pe.wait_ge(w_ready, w0 + 2)
                    for k in range(KT):
                        pe.wait_ge(h_lo, 8 * [1, 4][layer] + k + 1)
                        for n in range(4):
                            last = product(bank(n), w_tile(w0 + n // 2), h_cols(n % 2 * HALF, HALF), [k])
                            if k == KT - 1 and n % 2:
                                last.then_inc(up_ps, 1)

                def up_tile(slot, gv, pos, before, release=1):
                    pe.wait_ge(w_ready, pos + 1)
                    pe.wait_ge(cv2, before - 1)
                    for k in range(KT):
                        for hh in range(2):
                            last = product(bank(2 * gv + hh), w_tile(slot), h_cols(hh * HALF, HALF), [k],
                                           release=release if k == 0 and hh == 0 else 0)
                    last.then_inc(up_ps, 1)

                def down(slot, pos, hid_need, ev_need, ada_need):
                    pe.wait_ge(w_ready, pos + 2)
                    pe.wait_ge(hid_lo, hid_need)
                    if ada_need is not None:
                        pe.wait_ge(ada_ev, ada_need)
                    for m in range(8):
                        if m >= 2 or ev_need is not None:
                            pe.wait_ge(dn_ev, (ev_need if ev_need is not None else 88 * layer) + m - 1)
                        for hh in range(2):
                            for s in range(2):
                                for a, b in ((0, 0), (0, 1), (1, 0)):
                                    last = pe.matmul(bank(4 + 2 * (m % 2) + hh),
                                                     w_spl[:, (slot + s) % SPL, a, m * P:m * P + P],
                                                     hid[:, s, b, hh * HALF:hh * HALF + HALF],
                                                     start=(s == 0 and a + b == 0), stop=(s == 1 and a == 1))
                                    if m + hh + s + a + b == 0:
                                        last.then_inc(w_used, 1)
                        last.then_inc(dn_ps, 1)

                first_pair()
                up_tile(w0 + 2, 0, w0 + 2, u0 + 2, release=2)
                up_tile(w0 + 3, 1, w0 + 3, u0 + 3)

                def body(it, ada, ada_before):
                    pos = it * 6 + (w0 - 2)
                    ut = it * 4 + u0
                    up_tile(w0 - 2, 0, pos, ut)
                    up_tile(w0 - 1, 1, pos + 1, ut + 1)
                    down(w0, pos + 2, it * 2 + 22 * layer, it * 8 + (88 * layer - 8),
                         ada_before)
                    up_tile(w0 + 2, 0, pos + 4, ut + 2, release=2)
                    up_tile(w0 + 3, 1, pos + 5, ut + 3)
                    if ada:
                        pe.wait_ge(dn_ev, it * 8 + (88 * layer - 8) + 7)
                        ada_cols(ada_acc_f, 8, it * 8 + 64, 4, 0)

                def body1():
                    pos = w0 + 4
                    up_tile(w0 + 4, 0, pos, u0 + 4)
                    up_tile(w0 + 5, 1, pos + 1, u0 + 5)
                    down(w0, pos + 2, 22 * layer + 2, None, None)
                    up_tile(w0 + 2, 0, pos + 4, u0 + 6, release=2)
                    up_tile(w0 + 3, 1, pos + 5, u0 + 7)
                    if layer == 0:
                        pe.wait_ge(dn_ev, 7)
                        ada_cols(ada_acc_f, 8, 72, 4, 0)

                body1()
                if layer == 0:
                    with pe.Fori(2, 9) as it:
                        body(it, True, it + (N_ADA_A - 1))
                    for it in (9, 10):
                        body(it, False, N_ADA_A + 8)
                else:
                    with pe.Fori(0, 3) as third:
                        for r in range(3):
                            body(third * 3 + (r + 2), False, None)
                down(w0 + 64, w0 + 64, 22 * (layer + 1), 88 * layer + 80, None)

            out_proj(0)
            mean_squares(1, 1)
            ffn(0)
            mean_squares(2, 2)

            pe.wait_ge(w_ready, W_KV + 2)
            for k in range(KT):
                pe.wait_ge(h_lo, 16 + k + 1)
                for n in range(4):
                    last = product(bank(n), w_tile(W_KV + n // 2), h_cols((n % 2) * HALF, HALF), [k])
                    if k == KT - 1:
                        last.then_inc(kb_ps, 1)
            for k in range(KT):
                if k % 4 == 0:
                    pe.wait_ge(w_ready, W_KV + 3 + k // 4)
                for tt in range(8):
                    for a, b in ((0, 0), (0, 1), (1, 0)):
                        last = pe.matmul(bank(4 + tt // 2, tt % 2 * 256, tt % 2 * 256 + 256),
                                         H[:, k, a, tt * P:tt * P + P],
                                         w_spl[:, (W_KV + 2 + k // 4) % SPL, b, (k % 4) * 256:(k % 4) * 256 + 256],
                                         start=(k == 0 and a + b == 0 and tt % 2 == 0),
                                         stop=(k == KT - 1 and a == 1), skip_group_check=True)
                        if k % 4 == 0 and tt + a + b == 0:
                            last.then_inc(w_used, 1 if k else 2)
                last.then_inc(vk_ps, 1)

            def q_quarter(hp, qd):
                if qd == 0:
                    pe.wait_ge(w_ready, W_Q_B + hp + 1)
                if qd % 2 == 0 and 2 * hp + qd // 2 >= 2:
                    pe.wait_ge(qB_lo, 2 * hp + qd // 2 - 1)
                for k in range(4 * (qd % 2), 4 * (qd % 2) + 4):
                    if hp == 0 and qd < 2:
                        pe.wait_ge(h_lo, 24 + k + 1)
                    last = product(bank(q_bank(hp, qd // 2)), w_tile(W_Q_B + hp), h_cols(qd // 2 * HALF, HALF), [k],
                                   release=int(qd == 0 and k == 0))
                if qd % 2:
                    last.then_inc(qB_ps, 1)

            def scores_b(u):
                hp, qd = u // 4, u % 4
                if qd == 0:
                    pe.wait_ge(qB_lo, 2 * hp + 2)
                if u >= 2:
                    pe.wait_ge(sB_read, u - 1)
                for j in range(4):
                    n = 4 * qd + j
                    q = QB[:, hp % 2, n, :, :].rearrange("p e q -> p (e q)")
                    pe.matmul(bank(u % 2, j * P, j * P + P), q, KSB[:, hp // 2, n * CH:n * CH + P],
                              start=True, stop=False)
                    last = pe.matmul(bank(u % 2, j * P, j * P + P), q, KLB[:, hp // 2, n * CH:n * CH + P],
                                     start=False, stop=True)
                last.then_inc(sB_ps, 1)

            def turn_b(u):
                pe.wait_ge(pB, u + 1)
                if u >= 2:
                    pe.wait_ge(ptB_lo, u - 1)
                for j in range(4):
                    last = pe.transpose(bank(2 + u % 2, j * P, j * P + P), PB[u % 3][:, j, :], id_f[:])
                last.then_inc(tB_ps, 1)

            def values_b(u):
                hp, qd = u // 4, u % 4
                g = hp // 2
                pe.wait_ge(ptB_lo, u + 1)
                if u >= 2:
                    pe.wait_ge(o_addB, 2 * (u - 1))
                for j in range(4):
                    n = 4 * qd + j
                    v = (VB if n % 2 else VBs)[:, n // 2, g, :, :].rearrange("p a b -> p (a b)")
                    for part in range(2):
                        last = pe.matmul(bank(4 + u % 2, j * P, j * P + P), v, PTB[:, part, j * P:j * P + P],
                                         start=(part == 0), stop=(part == 1))
                last.then_inc(pvB_ps, 1)

            pe.wait_ge(kb_lo, 2)
            for qd in range(4):
                q_quarter(0, qd)
            pe.wait_ge(kb_lo, 8)
            q_quarter(1, 0)
            for u in range(35):
                if u < 32:
                    scores_b(u)
                if u == 3:
                    pe.wait_ge(vs_in, 48)
                if u >= 3:
                    values_b(u - 3)
                if 2 <= u <= 33:
                    turn_b(u - 2)
                if u < 27:
                    q_quarter((u + 1) // 4 + 1, (u + 1) % 4)
            out_proj(1)
            mean_squares(3, 1)
            ffn(1)
            mean_squares(4)

        @block.scalar
        def _(act):
            def squares(n):
                def one(k):
                    if n == 0:
                        act.wait_ge(x_in[k // 2], 16)
                    else:
                        s_, v_ = NORM_IN[n]
                        act.wait_ge(s_, v_ + k + 1)
                    if k >= 2:
                        act.wait_ge(ss_done, 8 * n + k - 1)
                    nc.scalar.activation(sq[:, k % 2], X[:, k], ACT.Square).then_inc(sq_done, 1)
                return one

            def root(n):
                act.wait_ge(ms_ps, n + 1)
                nc.scalar.activation(rt[:], bank(0, 0, 8), ACT.Sqrt, bias=eps_s[:], scale=1.0 / D).then_inc(rt_done, 1)

            def modulate(hn, used=None):
                sh = MODS[hn][2]
                for k in range(KT):
                    act.wait_ge(t_done, 8 * hn + k + 1)
                    if k >= 2:
                        act.wait_ge(h_lo, 8 * hn + k - 1)
                    a, b = coef[:, 8 * hn + k:8 * hn + k + 1], mods[:, sh + k:sh + k + 1]
                    nc.scalar.activation(hf[:, k % 2], tn[:, k % 2], ACT.Identity, scale=a, bias=b)
                    if used is not None:
                        act.wait_ge(used, k + 1)
                    nc.scalar.activation(H[:, k, 0], tn[:, k % 2], ACT.Identity, scale=a, bias=b).then_inc(h_hi, 1)

            act.wait_ge(const_in, 16 * 7)
            nc.scalar.activation(c_act[:], c_s[:], ACT.Silu).then_inc(cact_done, 1)
            act.wait_ge(set_done, 1)
            nc.scalar.activation(id_r[:], id_f[:], ACT.Copy)
            for k in range(8):
                squares(0)(k)
            root(0)
            act.wait_ge(gate_in, 48)
            nc.scalar.activation(mask_r[:], mask_f[:], ACT.Copy)
            nc.scalar.activation(wf[:, 0], wf_raw[:], ACT.Copy).then_inc(const_r, 1)
            modulate(0)
            act.wait_ge(z_v, 4)
            nc.scalar.activation(ze[:], za[:], ACT.Exp, scale=-1.0).then_inc(z_a, 1)
            act.wait_ge(z_a, 1)
            nc.scalar.activation(zl[:], ze[:], ACT.Ln, bias=one_s[:]).then_inc(z_a, 1)
            act.wait_ge(z_v, 7)
            act.dma_start(dF, nF16[:]).then_inc(f_out, 16)
            act.wait_ge(f_out, 16)

            with act.Fori(0, NG) as g:
                def load_negf(hl):
                    act.dma_start(negF[:, hl % 2, :], dF[bass.ds(g * 4 + hl, 1), :].partition_broadcast(P)[:, 0, :]
                                  ).then_inc(nf_in[hl % 2], 16)

                def load_ada(j):
                    act.dma_start(ada_raw_a[:], ada_w[0].rearrange("(k p) n -> p k n", p=P)[
                        :, :, bass.ds(g * 1024 + (2048 + 512 * j), 512)]).then_inc(ada_in, 16)

                def qk_high(n):
                    pp, is_k, hh = n // 4, n // 2 % 2, n % 2
                    act.wait_ge(qk_ps, g * 8 + (n + 1))
                    src = bank(n if n < 4 else PJ_BANK)
                    cols = slice(hh * HALF, hh * HALF + HALF)
                    for e in range(2):
                        rows = src[64 * e:64 * e + 64]
                        if is_k:
                            nc.scalar.activation(KS[pp][64:128, e, cols], rows, ACT.Copy)
                            last = nc.scalar.activation(KS[pp][0:64, e, cols], rows, ACT.Copy)
                        else:
                            last = nc.scalar.activation(QS[pp][0:64, e, cols], rows, ACT.Copy, scale=QSCALE)
                    last.then_inc(qk_hi, 1)

                load_ada(0)
                load_negf(0)
                load_negf(1)
                for n in range(4):
                    qk_high(n)
                    if n == 1:
                        act.wait_ge(ada_step, g * 16 + 8)
                        load_ada(1)
                for tt in range(8):
                    act.wait_ge(v_ps, g * 8 + (tt + 1))
                    nc.scalar.activation(V[:, tt, :, 0, :], bank(tt % 4, 0, 256).rearrange("p (h d) -> p h d", h=4),
                                         ACT.Copy).then_inc(v_hi, 1)
                def send_head(hl):
                    act.wait_ge(o_add, g * 16 + 4 * (hl + 1))
                    e = hl % 2
                    act.dma_start(dO[bass.ds(g * 2 + hl // 2, 1), 64 * e:64 * e + 64, :],
                                  O_st[64 * e:64 * e + 64, :]).then_inc(o_out[e], 16)

                for t in range(35):
                    if t % 8 == 4 and t > 4:
                        send_head((t - 12) // 8)
                    if 2 <= t <= 33:
                        tau = t - 2
                        i = tau % 8
                        for j in range(1 if i < 4 else 2):
                            act.wait_ge(t_ps, g * 48 + (tasks_to(tau) + j + 1))
                            if tau % 2 == 0 and tau >= 2 and j == 0:
                                act.wait_ge(pv_ps, g * 16 + tau // 2)
                            k0, k1 = 4 * j, min(4 * j + 4, i + 1)
                            nc.scalar.activation(
                                PT[:, 0, k0:k1, (tau % 2) * P:(tau % 2) * P + P],
                                bank(task_bank(tasks_to(tau) + j), 0, (k1 - k0) * P).rearrange("p (k q) -> p k q", q=P),
                                ACT.Copy).then_inc(pt_hi, 1)
                    if t < 32:
                        n = (t % 8 + 1) * P
                        act.wait_ge(s_max, g * 32 + (t + 1))
                        nc.scalar.activation(Pm[t % 3][:, 0:n], Pm[t % 3][:, 0:n], ACT.Exp,
                                             bias=nmx[:, t % 2:t % 2 + 1],
                                             accum_out=den[:, t % 2:t % 2 + 1]).then_inc(exp_done, 1)
                    if t % 2 == 0 and t >= 4:
                        q = (t - 4) // 2
                        e = q // 4 % 2
                        act.wait_ge(pv_ps, g * 16 + (q + 1))
                        if q:
                            act.wait_ge(o_add, g * 16 + q)
                        nc.scalar.activation(O_tmp[64 * e:64 * e + 64, :], bank(PV_BANK, 0, 256)[64 - 64 * e:128 - 64 * e],
                                             ACT.Copy).then_inc(o_tmp, 1)
                    if t < 16 and t % 4 == 3:
                        qk_high(4 + t // 4)
                    if t in (10, 18):
                        act.wait_ge(s_read, g * 32 + (t - 2))
                        load_negf(2 if t == 10 else 3)
                send_head(3)
                for e in range(2):
                    act.wait_ge(o_out[e], g * 32 + 32)

            def out_proj(layer, x_src):
                for e in range(2):
                    act.wait_ge(o_out[e], 16 * 8 * layer + 16 * 7)
                for k in range(4):
                    act.dma_start(O_raw[:, k], dO[k]).then_inc(o_in[k], 16)
                for k in range(8):
                    act.wait_ge(o_in[k % 4], 16 * (2 * layer + k // 4 + 1))
                    nc.scalar.activation(H[:, k, 0], O_raw[:, k % 4], ACT.Copy).then_inc(o_hi, 1)
                    if 1 <= k <= 4:
                        act.wait_ge(o_lo, 8 * layer + k)
                        if k == 4:
                            for e in range(2):
                                act.wait_ge(o_out[e], 16 * 8 * (layer + 1))
                        act.dma_start(O_raw[:, k - 1], dO[k + 3]).then_inc(o_in[k - 1], 16)
                for j in range(4):
                    act.dma_start(X[:, 2 * j:2 * j + 2], x_src.rearrange("k p s -> p k s")[
                        :, 2 * j:2 * j + 2]).then_inc(x_in[j], 16)

            def ffn(layer):
                u0, d0 = 2 * FT * layer, 88 * layer

                def tap(s, gv, tile, ut, low_need=None):
                    act.wait_ge(up_ps, ut + 1)
                    if low_need is not None:
                        act.wait_ge(hid_lo, low_need)
                    dst = (cG if gv == 0 else cV)[:, s]
                    par = conv_s[:, layer, :, :]
                    nc.scalar.activation(dst, pair(2 * gv), ACT.Identity, scale=par[:, tile, 2:3].rearrange("p a b -> p (a b)"),
                                         bias=par[:, tile, 3:4].rearrange("p a b -> p (a b)")).then_inc(cv0, 1)

                def silu(s, ut):
                    act.wait_ge(cv2, ut + 1)
                    nc.scalar.activation(cG[:, s], cG[:, s], ACT.Silu).then_inc(silu_done, 1)

                def high(s, jt, dn_need):
                    act.wait_ge(prod, jt + 1)
                    if dn_need is not None:
                        act.wait_ge(dn_ps, dn_need)
                    nc.scalar.activation(hid[:, s, 0], cV[:, s], ACT.Copy).then_inc(hid_hi, 1)

                def load_ada(chunk):
                    w_, n0 = chunk
                    act.dma_start(ada_raw_f[:], w_.rearrange("(k p) n -> p k n", p=P)[
                        :, :, bass.ds(n0, 1024)]).then_inc(ada_in, 16)

                def body(it, dn_need, ada):
                    for s in range(2):
                        ut = it * 4 + (u0 + 2 * s)
                        j = it * 2 + s
                        tap(s, 0, bass.ds(j, 1), ut)
                        silu(s, ut)
                        tap(s, 1, bass.ds(j + FT, 1), ut + 1,
                            None if dn_need is None else it * 2 + (FT * layer + s - 1))
                        high(s, it * 2 + (FT * layer + s), dn_need)
                        if s == 0 and ada is not None:
                            act.wait_ge(ada_step, ada[1])
                            load_ada(ada[0])

                if layer == 0:
                    act.wait_ge(h_lo, 16)
                    load_ada((kv_ada_w, 0))
                body(0, None, None)
                if layer == 0:
                    body(1, 8, ((kv_ada_w, 1024), 72))
                    with act.Fori(2, 8) as it:
                        body(it, it * 8, ((ada_w[1], it * 1024 - 2048), it * 8 + 64))
                    with act.Fori(8, 11) as it:
                        body(it, it * 8, None)
                else:
                    with act.Fori(1, 11) as it:
                        body(it, it * 8 + d0, None)

            out_proj(0, x_t)
            for k in range(8):
                squares(1)(k)
            root(1)
            modulate(1)
            ffn(0)
            for k in range(8):
                squares(2)(k)
            act.dma_start(dX.rearrange("k p s -> p k s"), X[:]).then_inc(x_out, 16)
            root(2)
            modulate(2)
            for n in range(4):
                act.wait_ge(kb_ps, n + 1)
                for e in range(2):
                    rows = bank(n)[64 * e:64 * e + 64]
                    gk = 2 * (n // 2) + e
                    cols = slice(PAD + n % 2 * HALF, PAD + n % 2 * HALF + HALF)
                    nc.scalar.activation(KSB[64:128, gk, cols], rows, ACT.Copy)
                    last = nc.scalar.activation(KSB[0:64, gk, cols], rows, ACT.Copy)
                last.then_inc(kb_hi, 1)
            modulate(3, vk_ps)
            act.wait_ge(vk_ps, 8)
            for b in range(4):
                nc.scalar.activation(VB[:, 2 * b:2 * b + 2, :, 0, :],
                                     bank(4 + b).rearrange("p (t h d) -> p t h d", t=2, h=4),
                                     ACT.Copy).then_inc(kb_hi, 1)
            act.wait_ge(x_out, 16)
            act.wait_ge(h_lo, 32)
            act.wait_ge(kb_lo, 8)
            act.dma_start(VBs[64:128].bitcast(F32), VB[0:64].bitcast(F32)).then_inc(vs_in, 16)
            act.dma_start(VBs[0:64, 1:8].bitcast(F32), VB[64:128, 0:7].bitcast(F32)).then_inc(vs_in, 16)
            act.dma_start(bias_s[:], alibi).then_inc(vs_in, 16)

            def q_high(hp, hh):
                act.wait_ge(qB_ps, 2 * hp + hh + 1)
                for e in range(2):
                    rows = bank(q_bank(hp, hh))[64 * e:64 * e + 64].rearrange("p (n q) -> p n q", q=CH)
                    last = nc.scalar.activation(QB[0:64, hp % 2, 8 * hh:8 * hh + 8, e, :], rows, ACT.Copy,
                                                scale=QSCALE)
                last.then_inc(qB_hi, 1)

            q_high(0, 0)
            q_high(0, 1)
            def send_pair(hp):
                act.wait_ge(o_addB, 8 * hp + 8)
                for e in range(2):
                    act.dma_start(dO[hp, 64 * e:64 * e + 64, :], O_stB[64 * e:64 * e + 64]).then_inc(o_out[e], 16)

            for u in range(35):
                if u >= 8 and u % 4 == 0:
                    send_pair(u // 4 - 2)
                if 2 <= u <= 33:
                    act.wait_ge(tB_ps, u - 1)
                    if u >= 3:
                        act.wait_ge(pvB_ps, u - 2)
                    nc.scalar.activation(PTB[:, 0], bank(2 + u % 2), ACT.Copy).then_inc(ptB_hi, 1)
                if u < 32:
                    hp = u // 4
                    act.wait_ge(mB, u + 1)
                    for j in range(4):
                        nc.scalar.activation(PB[u % 3][:, j, :], PB[u % 3][:, j, :], ACT.Exp,
                                             bias=nmB[:, u % 2, j:j + 1], accum_out=dnB[:, u % 2, j:j + 1])
                    nc.scalar.activation(esB[:, u % 2], nmB[:, u % 2], ACT.Exp,
                                         bias=sink_s[:, hp:hp + 1]).then_inc(expB, 1)
                if u >= 3:
                    v = u - 3
                    act.wait_ge(pvB_ps, v + 1)
                    for e in range(2):
                        if 2 * v + e >= 2:
                            act.wait_ge(o_addB, 2 * v + e - 1)
                        src = bank(4 + v % 2)[64 - 64 * e:128 - 64 * e].rearrange("p (n e q) -> p n e q", e=2, q=CH)
                        nc.scalar.activation(O_tmpB[64 * e:64 * e + 64], src[:, :, e, :], ACT.Copy).then_inc(o_tmpB, 1)
                if u < 27 and u % 2 == 0:
                    q_high((u + 1) // 4 + 1, (u + 1) % 4 // 2)
            send_pair(7)

            out_proj(1, dX)
            for k in range(8):
                squares(3)(k)
            root(3)
            modulate(4)
            ffn(1)
            for k in range(8):
                squares(4)(k)
            root(4)
            for k in range(8):
                act.wait_ge(t_done, 40 + k + 1)
                if k >= 2:
                    act.wait_ge(y_out[k % 2], 16 * (k // 2))
                nc.scalar.activation(hf[:, k % 2], tn[:, k % 2], ACT.Copy,
                                     scale=gain[:, G_FIN + k:G_FIN + k + 1]).then_inc(y_done, 1)
                act.wait_ge(y_done, k + 1)
                act.dma_start(out_t[k], hf[:, k % 2]).then_inc(y_out[k % 2], 16)
            for e in range(2):
                act.wait_ge(y_out[e], 64)

        @block.vector
        def _(dve):
            V_ = nc.vector

            def add_squares(n):
                def one(k):
                    dve.wait_ge(sq_done, 8 * n + k + 1)
                    if k == 0:
                        V_.tensor_copy(ss[:], sq[:, 0]).then_inc(ss_done, 1)
                    else:
                        dve.wait_ge(ss_done, 8 * n + k)
                        V_.tensor_tensor(ss[:], ss[:], sq[:, k % 2], ALU.add).then_inc(ss_done, 1)
                return one

            def inverse_root(n):
                dve.wait_ge(rt_done, n + 1)
                V_.reciprocal(rs[:], rt[:]).then_inc(rs_done, 1)
                dve.wait_ge(rs_done, 3 * n + 1)
                V_.tensor_tensor(diag[:], id_f[:, None, :].to_broadcast([P, KT, P]),
                                 rs[:, :, None].to_broadcast([P, KT, P]), ALU.mult).then_inc(rs_done, 1)
                dve.wait_ge(bc_ps, n + 1)
                V_.tensor_copy(rstd[:], pair(0)).then_inc(rs_done, 1)
                dve.wait_ge(rs_done, 3 * n + 3)

            def coefficients(hn):
                gc, sc, _ = MODS[hn]
                V_.scalar_tensor_tensor(coef[:, 8 * hn:8 * hn + 8], mods[:, sc:sc + 8], 1.0, gain[:, gc:gc + 8],
                                        ALU.add, ALU.mult)

            def scaled(hn, k, free):
                if k >= 2:
                    dve.wait_ge(free, (8 * hn if hn < 5 else 0) + k - 1)
                V_.tensor_tensor(tn[:, k % 2], X[:, k], rstd[:], ALU.mult).then_inc(t_done, 1)

            def low(hn, k):
                dve.wait_ge(h_hi, 8 * hn + k + 1)
                V_.tensor_tensor(H[:, k, 1], hf[:, k % 2], H[:, k, 0].bitcast(F32), ALU.subtract).then_inc(h_lo, 1)

            def modulate(hn):
                for k in range(KT + 1):
                    if k < KT:
                        scaled(hn, k, h_hi)
                    if k:
                        low(hn, k - 1)

            def ada_steps(acc, raw, first, ks=range(KT), steps=ada_step):
                for k in ks:
                    if k == 0:
                        V_.tensor_scalar(acc, raw(k), c_act[:, 0:1], None, ALU.mult).then_inc(steps, 1)
                    else:
                        dve.wait_ge(steps, first + k)
                        V_.scalar_tensor_tensor(acc, raw(k), c_act[:, k:k + 1], acc, ALU.mult,
                                                ALU.add).then_inc(steps, 1)

            V_.memset(eps_s[:], EPS)
            V_.memset(one_s[:], 1.0)
            V_.memset(ones[:], 1.0).then_inc(set_done, 1)
            for k in range(8):
                add_squares(0)(k)
            inverse_root(0)
            dve.wait_ge(const_r, 1)
            V_.tensor_tensor(wf[:, 1], wf_raw[:], wf[:, 0].bitcast(F32), ALU.subtract).then_inc(z_v, 1)
            dve.wait_ge(cact_done, 1)
            for j in range(4):
                dve.wait_ge(ada0_in[j], 16)
                ada_steps(ada_acc0[:, j], lambda k: ada_raw0[:, j, k, :], 8 * j, steps=ada0_step)
                dve.wait_ge(ada_ps, j + 1)
                V_.tensor_tensor(mods[:, 4 * j:4 * j + 4], bank(PV_BANK, 0, 4), modb[:, 4 * j:4 * j + 4],
                                 ALU.add).then_inc(ada_ev, 1)
            dve.wait_ge(ada_ev, 4)
            coefficients(0)
            modulate(0)
            dve.wait_ge(z_ps, 1)
            V_.tensor_copy(zt[:], BK[0][0:16, 2:4, :].rearrange("p a b -> p (a b)")).then_inc(z_v, 1)
            dve.wait_ge(z_ps, 2)
            V_.tensor_tensor(zb[:], bank(4, 0, 128).rearrange("p (t h) -> p t h", h=16),
                             bf_s[:, None, :].to_broadcast([P, 8, 16]), ALU.add).then_inc(z_v, 1)
            dve.wait_ge(z_v, 3)
            V_.scalar_tensor_tensor(za[:], zb[:], -1.0, zb[:], ALU.mult, ALU.max).then_inc(z_v, 1)
            dve.wait_ge(z_v, 4)
            V_.tensor_scalar(zb[:], zb[:], 0.0, None, ALU.min).then_inc(z_v, 1)
            dve.wait_ge(z_v, 5)
            dve.wait_ge(z_a, 2)
            V_.tensor_tensor(lf[:], zb[:], zl[:], ALU.subtract).then_inc(z_v, 1)
            dve.wait_ge(f_ps, 1)
            V_.tensor_scalar(nF16[:], BK[0][0:16, 0:2, :].rearrange("p a b -> p (a b)"), -1.0, None,
                             ALU.mult).then_inc(z_v, 1)
            dve.wait_ge(f_out, 16)
            for b in range(2):
                V_.memset(KL[b][64:128].bitcast(F32), 0.0)

            with dve.Fori(0, NG) as g:
                def qk_low(n):
                    pp, is_k, hh = n // 4, n // 2 % 2, n % 2
                    dve.wait_ge(qk_hi, g * 8 + (n + 1))
                    src = bank(n if n < 4 else PJ_BANK)
                    cols = slice(hh * HALF, hh * HALF + HALF)
                    for e in range(2):
                        rows = src[64 * e:64 * e + 64]
                        if is_k:
                            last = V_.tensor_tensor(KL[pp][0:64, e, cols], rows, KS[pp][0:64, e, cols].bitcast(F32),
                                                    ALU.subtract)
                        else:
                            last = V_.scalar_tensor_tensor(QS[pp][64:128, e, cols], rows, QSCALE,
                                                           QS[pp][0:64, e, cols].bitcast(F32), ALU.mult, ALU.subtract)
                    last.then_inc(qk_lo, 1)

                def v_low(tt):
                    dve.wait_ge(v_hi, g * 8 + (tt + 1))
                    V_.tensor_tensor(V[:, tt, :, 1, :], bank(tt % 4, 0, 256).rearrange("p (h d) -> p h d", h=4),
                                     V[:, tt, :, 0, :].bitcast(F32), ALU.subtract).then_inc(v_lo, 1)

                def ada_piece(j):
                    dve.wait_ge(ada_in, g * 32 + 16 * (j + 1))
                    ada_steps(ada_acc_a[:, j], lambda k: ada_raw_a[:, k, :], g * 16 + 8 * j)

                qk_low(0)
                ada_piece(0)
                for n in range(1, 4):
                    qk_low(n)
                for tt in range(8):
                    v_low(tt)
                    if tt == 4:
                        ada_piece(1)
                dve.wait_ge(ada_ps, g * 2 + 6)
                for j in range(2):
                    V_.tensor_tensor(mods[:, bass.ds(g * 8 + (16 + 4 * j), 4)], bank(PV_BANK, 4 * j, 4 * j + 4),
                                     modb[:, bass.ds(g * 8 + (16 + 4 * j), 4)], ALU.add).then_inc(ada_ev, 1)

                for t in range(36):
                    if t % 4 == 0 and 4 <= t <= 16:
                        qk_low(3 + t // 4)
                    if t < 32:
                        hl = t // 8
                        n = (t % 8 + 1) * P
                        dve.wait_ge(s_ps, g * 32 + (t + 1))
                        if t >= 3:
                            dve.wait_ge(t_ps, g * 48 + tasks_to(t - 2))
                        if t % 8 == 0:
                            dve.wait_ge(nf_in[hl % 2], g * 32 + 16 * (hl // 2 + 1))
                        V_.tensor_copy(pace[:, 1:2], one_s[:])
                        V_.tensor_tensor_reduce(Pm[t % 3][:, 0:n], pair(2 * (t % 2))[:, 0:n], negF[:, hl % 2, 0:n], 1.0,
                                                NEG, ALU.add, ALU.max, mx[:, t % 2:t % 2 + 1]).then_inc(s_read, 1)
                        dve.wait_ge(s_read, g * 32 + (t + 1))
                        V_.tensor_scalar(nmx[:, t % 2:t % 2 + 1], mx[:, t % 2:t % 2 + 1], -1.0, None,
                                         ALU.mult).then_inc(s_max, 1)
                    if 1 <= t <= 32:
                        tau = t - 1
                        n = (tau % 8 + 1) * P
                        dve.wait_ge(exp_done, g * 32 + t)
                        V_.reciprocal(rden[:, tau % 2:tau % 2 + 1], den[:, tau % 2:tau % 2 + 1]).then_inc(rd_done, 1)
                        dve.wait_ge(rd_done, g * 32 + t)
                        V_.tensor_scalar(Pm[tau % 3][:, 0:n], Pm[tau % 3][:, 0:n], rden[:, tau % 2:tau % 2 + 1], None,
                                         ALU.mult).then_inc(p_norm, 1)
                    if t % 2 and t >= 5:
                        q = (t - 5) // 2
                        e, c = q // 4 % 2, q % 4
                        dve.wait_ge(o_tmp, g * 16 + (q + 1))
                        if q == 8 or q == 12:
                            dve.wait_ge(o_out[e], g * 32 + 16)
                        V_.tensor_tensor(O_st[64 * e:64 * e + 64, c * 256:c * 256 + 256],
                                         bank(PV_BANK, 0, 256)[64 * e:64 * e + 64], O_tmp[64 * e:64 * e + 64],
                                         ALU.add).then_inc(o_add, 1)
                    if 2 <= t <= 33:
                        tau = t - 2
                        i = tau % 8
                        for j in range(1 if i < 4 else 2):
                            dve.wait_ge(pt_hi, g * 48 + (tasks_to(tau) + j + 1))
                            k0, k1 = 4 * j, min(4 * j + 4, i + 1)
                            cols = slice((tau % 2) * P, (tau % 2) * P + P)
                            V_.tensor_tensor(PT[:, 1, k0:k1, cols],
                                             bank(task_bank(tasks_to(tau) + j), 0, (k1 - k0) * P).rearrange("p (k q) -> p k q", q=P),
                                             PT[:, 0, k0:k1, cols].bitcast(F32), ALU.subtract).then_inc(pt_lo, 1)

            def out_proj(layer):
                n = 1 + 2 * layer
                gc = M_G1 + M_L1 * layer
                for k in range(8):
                    dve.wait_ge(o_hi, 8 * layer + k + 1)
                    V_.tensor_tensor(H[:, k, 1], O_raw[:, k % 4], H[:, k, 0].bitcast(F32),
                                     ALU.subtract).then_inc(o_lo, 1)
                for m in range(8):
                    dve.wait_ge(wo_ps, 8 * layer + m + 1)
                    dve.wait_ge(x_in[m // 2], 32 + 16 * layer)
                    V_.scalar_tensor_tensor(X[:, m], pair(4 + 2 * (m % 2)), mods[:, gc + m:gc + m + 1], X[:, m],
                                            ALU.mult, ALU.add).then_inc(wo_ev, 1)
                    if m:
                        add_squares(n)(m - 1)
                add_squares(n)(7)

            def ffn(layer):
                u0, d0, gc = 2 * FT * layer, 88 * layer, M_G2 + M_L1 * layer

                def taps(s, gv, tile, ut):
                    dst = (cG if gv == 0 else cV)[:, s]
                    src = pair(2 * gv)
                    par = conv_s[:, layer, :, :]
                    dve.wait_ge(cv0, ut + 1)
                    V_.scalar_tensor_tensor(dst[:, 1:S], src[:, 0:S - 1], par[:, tile, 1:2].rearrange("p a b -> p (a b)"),
                                            dst[:, 1:S], ALU.mult, ALU.add).then_inc(cv1, 1)
                    dve.wait_ge(cv1, ut + 1)
                    V_.scalar_tensor_tensor(dst[:, 2:S], src[:, 0:S - 2], par[:, tile, 0:1].rearrange("p a b -> p (a b)"),
                                            dst[:, 2:S], ALU.mult, ALU.add).then_inc(cv2, 1)

                def gated(s, ut, jt):
                    dve.wait_ge(silu_done, jt + 1)
                    dve.wait_ge(cv2, ut + 2)
                    V_.tensor_tensor(cV[:, s], cV[:, s], cG[:, s], ALU.mult).then_inc(prod, 1)

                def low_part(s, jt):
                    dve.wait_ge(hid_hi, jt + 1)
                    V_.tensor_tensor(hid[:, s, 1], cV[:, s], hid[:, s, 0].bitcast(F32), ALU.subtract).then_inc(hid_lo, 1)

                def residual(m, ps_need, self_need):
                    dve.wait_ge(dn_ps, ps_need)
                    if self_need is not None:
                        dve.wait_ge(dn_ev, self_need)
                    V_.scalar_tensor_tensor(X[:, m], pair(4 + 2 * (m % 2)), mods[:, gc + m:gc + m + 1], X[:, m],
                                            ALU.mult, ALU.add).then_inc(dn_ev, 1)

                def body(it, with_down, first_down, ada):
                    for s in range(2):
                        ut = it * 4 + (u0 + 2 * s)
                        j = it * 2 + s
                        jt = it * 2 + (FT * layer + s)
                        taps(s, 0, bass.ds(j, 1), ut)
                        taps(s, 1, bass.ds(j + FT, 1), ut + 1)
                        gated(s, ut, jt)
                        if s == 0 and with_down:
                            if ada is not None:
                                dve.wait_ge(ada_in, ada[0])
                            for m in range(8):
                                need = it * 8 + (d0 - 8 + m + 1)
                                residual(m, need, None if first_down else need - 8)
                                if ada is not None:
                                    ada_steps(ada_acc_f[:], lambda k: ada_raw_f[:, k, :], ada[1], ks=[m])
                        if s == 1 and ada is not None:
                            dve.wait_ge(ada_ps, ada[2])
                            V_.tensor_tensor(mods[:, ada[3]], bank(4, 0, 8), modb[:, ada[3]], ALU.add).then_inc(ada_ev, 1)
                        low_part(s, jt)

                def ada_of(it, cols):
                    return (it * 16 + 128, it * 8 + 56, it + N_ADA_A, cols)

                body(0, False, False, None)
                if layer == 0:
                    body(1, True, True, ada_of(1, slice(M_KV, M_KV + 8)))
                    body(2, True, False, ada_of(2, slice(M_KV + 8, M_KV + 16)))
                    with dve.Fori(3, 9) as it:
                        body(it, True, False, ada_of(it, bass.ds(it * 8 + (M_L1 - 24), 8)))
                    with dve.Fori(9, 11) as it:
                        body(it, True, False, None)
                else:
                    body(1, True, True, None)
                    with dve.Fori(2, 11) as it:
                        body(it, True, False, None)
                for m in range(8):
                    residual(m, d0 + 80 + m + 1, d0 + 72 + m + 1)
                    if m:
                        add_squares(2 + 2 * layer)(m - 1)
                add_squares(2 + 2 * layer)(7)

            out_proj(0)
            dve.wait_ge(ada_ev, N_ADA_A)
            coefficients(1)
            inverse_root(1)
            modulate(1)
            ffn(0)
            dve.wait_ge(ada_ev, N_ADA_A + 8)
            coefficients(2)
            coefficients(3)
            inverse_root(2)
            modulate(2)
            V_.memset(KSB[:, :, 0:PAD].bitcast(F32), 0.0)
            V_.memset(KLB[0:64, :, 0:PAD].bitcast(F32), 0.0)
            V_.memset(KLB[64:128].bitcast(F32), 0.0)
            for n in range(4):
                dve.wait_ge(kb_hi, n + 1)
                for e in range(2):
                    gk = 2 * (n // 2) + e
                    cols = slice(PAD + n % 2 * HALF, PAD + n % 2 * HALF + HALF)
                    last = V_.tensor_tensor(KLB[0:64, gk, cols], bank(n)[64 * e:64 * e + 64],
                                            KSB[0:64, gk, cols].bitcast(F32), ALU.subtract)
                last.then_inc(kb_lo, 1)
            modulate(3)
            for b in range(4):
                dve.wait_ge(kb_hi, 4 + b + 1)
                V_.tensor_tensor(VB[:, 2 * b:2 * b + 2, :, 1, :],
                                 bank(4 + b).rearrange("p (t h d) -> p t h d", t=2, h=4),
                                 VB[:, 2 * b:2 * b + 2, :, 0, :].bitcast(F32), ALU.subtract).then_inc(kb_lo, 1)
            dve.wait_ge(x_out, 16)
            V_.memset(VBs[0:64, 0].bitcast(F32), 0.0)

            def q_low(hp, hh):
                dve.wait_ge(qB_hi, 2 * hp + hh + 1)
                ch = slice(8 * hh, 8 * hh + 8)
                for e in range(2):
                    rows = bank(q_bank(hp, hh))[64 * e:64 * e + 64].rearrange("p (n q) -> p n q", q=CH)
                    last = V_.scalar_tensor_tensor(QB[64:128, hp % 2, ch, e, :], rows, QSCALE,
                                                   QB[0:64, hp % 2, ch, e, :].bitcast(F32), ALU.mult, ALU.subtract)
                last.then_inc(qB_lo, 1)

            q_low(0, 0)
            q_low(0, 1)
            dve.wait_ge(vs_in, 48)
            for u in range(36):
                if u <= 27 and u % 2:
                    q_low(u // 4 + 1, u % 4 // 2)
                if u < 32:
                    b, hp = u % 2, u // 4
                    dve.wait_ge(sB_ps, u + 1)
                    if u >= 3:
                        dve.wait_ge(tB_ps, u - 2)
                    for j in range(4):
                        if u % 4 == 0 and j == 0:
                            V_.memset(PB[u % 3][:, 0, 0:CH], NEG)
                            last = V_.tensor_tensor_reduce(PB[u % 3][:, j, CH:P], bank(b, CH, P), bias_s[:, hp, CH:P],
                                                           1.0, NEG, ALU.add, ALU.max, mxB[:, b, j:j + 1])
                        else:
                            last = V_.tensor_tensor_reduce(PB[u % 3][:, j, :], bank(b, j * P, j * P + P), bias_s[:, hp, :],
                                                           1.0, NEG, ALU.add, ALU.max, mxB[:, b, j:j + 1])
                    last.then_inc(sB_read, 1)
                    dve.wait_ge(sB_read, u + 1)
                    V_.tensor_scalar(nmB[:, b], mxB[:, b], sink_s[:, hp:hp + 1], -1.0, ALU.max, ALU.mult).then_inc(mB, 1)
                if 1 <= u <= 32:
                    v = u - 1
                    b = v % 2
                    dve.wait_ge(expB, v + 1)
                    V_.tensor_tensor(dnB[:, b], dnB[:, b], esB[:, b], ALU.add).then_inc(dB, 1)
                    dve.wait_ge(dB, 2 * v + 1)
                    V_.reciprocal(rdB[:, b], dnB[:, b]).then_inc(dB, 1)
                    dve.wait_ge(dB, 2 * v + 2)
                    V_.tensor_tensor(PB[v % 3][:], PB[v % 3][:], rdB[:, b, :, None].to_broadcast([P, 4, P]),
                                     ALU.mult).then_inc(pB, 1)
                if u >= 4:
                    v = u - 4
                    if v % 4 == 0 and v:
                        for e in range(2):
                            dve.wait_ge(o_out[e], 128 + 16 * (v // 4))
                    dve.wait_ge(o_tmpB, 2 * v + 2)
                    for e in range(2):
                        src = bank(4 + v % 2)[64 * e:64 * e + 64].rearrange("p (n e q) -> p n e q", e=2, q=CH)
                        dst = O_stB[64 * e:64 * e + 64, v % 4 * 256:v % 4 * 256 + 256].rearrange("p (n q) -> p n q", q=CH)
                        V_.tensor_tensor(dst, src[:, :, e, :], O_tmpB[64 * e:64 * e + 64], ALU.add).then_inc(o_addB, 1)
                if 2 <= u <= 33:
                    dve.wait_ge(ptB_hi, u - 1)
                    V_.tensor_tensor(PTB[:, 1], bank(2 + u % 2), PTB[:, 0].bitcast(F32),
                                     ALU.subtract).then_inc(ptB_lo, 1)

            out_proj(1)
            coefficients(4)
            inverse_root(3)
            modulate(4)
            ffn(1)
            inverse_root(4)
            for k in range(8):
                scaled(5, k, y_done)


INPUTS = ["x_t", "c_t", "ada_w", "kv_ada_w", "mod_b", "gains", "w_stream", "w_f", "b_f", "sinks", "conv",
          "ident", "mask", "stair", "alibi"]


def layout(i):
    f = np.float32
    a = {k: np.asarray(v) for k, v in i.items()}

    def stationary(w, m):
        return w[:, m * P:m * P + P].reshape(KT, P, P).transpose(1, 0, 2).reshape(P, 1024)

    def moving(w, n0):
        t = w[:, n0:n0 + 256].reshape(2, 4, P, 256).transpose(0, 2, 1, 3).reshape(2, P, 1024)
        return [t[0], t[1]]

    w_in = a["a_w_in"][0]
    wq, wk, wv = w_in[:, 0:D], w_in[:, D:2 * D], w_in[:, 2 * D:3 * D]
    tiles = []
    for g in range(NG):
        tiles += [stationary(wq, 2 * g), stationary(wk, 2 * g)]
        tiles += moving(wv, 256 * g)
        tiles += [stationary(wq, 2 * g + 1), stationary(wk, 2 * g + 1)]
    tiles += [stationary(a["a_w_o"][0], m) for m in range(8)]

    def ffn(l):
        up, dn = a["ffn_w_up"][l], a["ffn_w_down"][l]
        ups = lambda j: [stationary(up, j), stationary(up, FT + j)]
        out = ups(0) + ups(1)
        for it in range(1, FT // 2):
            out += ups(2 * it) + [dn[(2 * it - 2) * P:(2 * it - 1) * P], dn[(2 * it - 1) * P:2 * it * P]] + ups(2 * it + 1)
        return out + [dn[(FT - 2) * P:(FT - 1) * P], dn[(FT - 1) * P:]]

    tiles += ffn(0)
    tiles += [stationary(a["kv_w"], m) for m in range(2)] + moving(a["kv_w"], KV * HD)
    tiles += [stationary(a["b_w_q"][0], m) for m in range(8)]
    tiles += [stationary(a["b_w_o"][0], m) for m in range(8)]
    tiles += ffn(1)
    cols = lambda v: np.asarray(v).reshape(-1, P).T
    conv = np.stack([np.stack([cols(a["ffn_conv_w"][l][j]) for j in range(3)] + [cols(a["ffn_conv_b"][l])], axis=-1)
                     for l in range(2)], axis=1)
    r = np.arange(P)
    mask = np.where(r[None, :] <= r[:, None], 0.0, NEG).astype(f)
    stair = (np.arange(S)[None, :] >= r[:, None]).astype(f)
    slopes = np.exp2(-8.0 * (np.arange(NH, dtype=f) + 1.0) / NH).astype(f)
    dist = np.abs(np.arange(CH)[:, None] + CH - np.arange(2 * CH)[None, :]).astype(f)
    alibi = -(slopes.reshape(8, 2)[:, :, None, None] * dist[None, None]).reshape(8, P, P).transpose(1, 0, 2)
    return {
        "x_t": a["x"][0].T.reshape(KT, P, S), "c_t": cols(a["c"][0]), "ada_w": a["ada_w"],
        "kv_ada_w": a["kv_ada_w"],
        "mod_b": np.concatenate([cols(a["ada_b"][0]), cols(a["ada_b"][1]), cols(a["kv_ada_b"])], axis=1),
        "gains": np.concatenate([cols(v) for v in (a["norm1_g"][0], a["norm1_g"][1], a["norm2_g"][0],
                                                   a["norm2_g"][1], a["kv_norm_g"], a["final_g"])], axis=1),
        "w_stream": np.stack(tiles), "w_f": w_in[:, 3 * D:].reshape(KT, P, NH).transpose(1, 0, 2),
        "b_f": np.broadcast_to(a["a_b_f"][0], (P, NH)),
        "sinks": np.repeat(a["b_sinks"][0].reshape(8, 2).T, CH, axis=0),
        "conv": conv, "ident": np.eye(P, dtype=f), "mask": mask, "stair": stair, "alibi": alibi,
    }


def kernel(**inputs):
    import concourse.bacc as bacc
    from concourse.bass_utils import run_bass_kernel_spmd as run

    nc = bacc.Bacc("TRN2", target_bir_lowering=False, num_devices=1)
    arrays, args = {}, []
    laid = layout(inputs)
    for name in INPUTS:
        v = np.ascontiguousarray(laid[name])
        arrays[f"in_{name}"] = v
        args.append(nc.dram_tensor(f"in_{name}", v.shape, mybir.dt.from_np(v.dtype), kind="ExternalInput").ap())
    args.append(nc.dram_tensor("out_0", (KT, P, S), F32, kind="ExternalOutput").ap())
    program(nc, *args)
    r = run(nc, [arrays], core_ids=[0])
    return r.results[0]["out_0"].reshape(D, S).T.reshape(1, S, D)
```
